# Optimizing a Trainium2 kernel written in Bass

```python
import jax, jax.numpy as jnp
from jax import lax
import numpy as np

D_MODEL = 1024
BATCH = 1
SEQ = 256
DEPTH = 1

N_Q_HEADS = 16
N_KV_HEADS = 2
HEAD_DIM = 64
Q_PER_KV = N_Q_HEADS // N_KV_HEADS
WINDOW = 128
BLOCK = 128
ROPE_THETA = 500000.0
ROPE_DIM = HEAD_DIM // 4
ATTN_W = N_Q_HEADS * HEAD_DIM
KV_W = N_KV_HEADS * HEAD_DIM
CONV_CH = D_MODEL
CONV_WIDTH = 31
D_FF = 2816
PLE_DIM = 256
EPS = 1e-6
NEG_INF = -1e30
SPLIT_SIZES = (ATTN_W, KV_W, KV_W, 2 * CONV_CH, 2 * D_MODEL)
D_IN = sum(SPLIT_SIZES)


def rmsnorm(x, g):
    xf = x.astype(jnp.float32)
    y = xf * lax.rsqrt(jnp.mean(xf * xf, axis=-1, keepdims=True) + EPS) * g.astype(jnp.float32)
    return y.astype(x.dtype)

def layernorm(x, g, b):
    xf = x.astype(jnp.float32)
    mu = jnp.mean(xf, axis=-1, keepdims=True)
    xc = xf - mu
    var = jnp.mean(xc * xc, axis=-1, keepdims=True)
    y = xc * lax.rsqrt(var + EPS) * g.astype(jnp.float32) + b.astype(jnp.float32)
    return y.astype(x.dtype)

def swiglu(h, w_gu, w_down):
    g, u = jnp.split(h @ w_gu, 2, axis=-1)
    return (jax.nn.silu(g) * u) @ w_down

def partial_rope(t, cos, sin):
    half = ROPE_DIM // 2
    t1 = t[..., :half]
    t2 = t[..., half:ROPE_DIM]
    rot = jnp.concatenate([t1 * cos - t2 * sin, t2 * cos + t1 * sin], axis=-1)
    return jnp.concatenate([rot.astype(t.dtype), t[..., ROPE_DIM:]], axis=-1)

def rope_tables(seq):
    inv_freq = ROPE_THETA ** (-jnp.arange(0, ROPE_DIM, 2, dtype=jnp.float32) / ROPE_DIM)
    ang = jnp.arange(seq, dtype=jnp.float32)[:, None] * inv_freq[None, :]
    return jnp.cos(ang)[None, :, None, :], jnp.sin(ang)[None, :, None, :]

def sliding_window_attention(q, k, v, sinks):
    B, S = q.shape[0], q.shape[1]
    nb = S // BLOCK
    qb = q.reshape(B, nb, BLOCK, N_KV_HEADS, Q_PER_KV, HEAD_DIM)

    def band(t):
        tb = t.reshape(B, nb, BLOCK, N_KV_HEADS, HEAD_DIM)
        prev = jnp.concatenate([jnp.zeros_like(tb[:, :1]), tb[:, :-1]], axis=1)
        return jnp.concatenate([prev, tb], axis=2)

    kb, vb = band(k), band(v)
    scale = HEAD_DIM ** -0.5
    s = jnp.einsum('bnqhgd,bnkhd->bnhgqk', qb, kb,
                   preferred_element_type=jnp.float32) * scale
    qi = jnp.arange(BLOCK)[:, None]
    kj = jnp.arange(2 * BLOCK)[None, :]
    delta = qi + BLOCK - kj
    kpos = jnp.arange(nb)[:, None, None] * BLOCK + kj[None] - BLOCK
    valid = (delta >= 0) & (delta < WINDOW) & (kpos >= 0)
    s = jnp.where(valid[None, :, None, None], s, NEG_INF)
    sink = sinks.astype(jnp.float32).reshape(N_KV_HEADS, Q_PER_KV)[None, None, :, :, None, None]
    m = jnp.maximum(jnp.max(s, axis=-1, keepdims=True), sink)
    pr = jnp.exp(s - m)
    denom = jnp.sum(pr, axis=-1, keepdims=True) + jnp.exp(sink - m)
    o = jnp.einsum('bnhgqk,bnkhd->bnqhgd', pr / denom, vb.astype(jnp.float32))
    return o.reshape(B, S, ATTN_W).astype(q.dtype)

def causal_depthwise_conv(u, w_dw, b_dw):
    up = jnp.pad(u, ((0, 0), (CONV_WIDTH - 1, 0), (0, 0)))
    y = lax.conv_general_dilated(up, w_dw[:, None, :], window_strides=(1,), padding='VALID',
                                 dimension_numbers=('NWC', 'WIO', 'NWC'),
                                 feature_group_count=CONV_CH)
    return y + b_dw

def first_inputs(seed: int = 0) -> dict:
    key = jax.random.key(seed)
    ks = jax.random.split(key, 32)

    def nrm(k, shape, scale):
        return jax.random.normal(k, shape, jnp.float32) * scale

    def gain(k, shape):
        return 1.0 + 0.05 * jax.random.normal(k, shape, jnp.float32)

    L = DEPTH
    return {
        "x": nrm(ks[0], (BATCH, SEQ, D_MODEL), 1.0),
        "p": nrm(ks[1], (DEPTH, BATCH, SEQ, PLE_DIM), 1.0),
        "ffn1_norm": gain(ks[2], (L, D_MODEL)),
        "ffn1_wgu": nrm(ks[3], (L, D_MODEL, 2 * D_FF), D_MODEL ** -0.5),
        "ffn1_wdown": nrm(ks[4], (L, D_FF, D_MODEL), D_FF ** -0.5),
        "mix_norm": gain(ks[5], (L, D_MODEL)),
        "w_in": nrm(ks[6], (L, D_MODEL, D_IN), D_MODEL ** -0.5),
        "q_norm": gain(ks[7], (L, HEAD_DIM)),
        "k_norm": gain(ks[8], (L, HEAD_DIM)),
        "sinks": nrm(ks[9], (L, N_Q_HEADS), 0.5),
        "attn_proj": nrm(ks[10], (L, ATTN_W, D_MODEL), ATTN_W ** -0.5),
        "dw_w": nrm(ks[11], (L, CONV_WIDTH, CONV_CH), CONV_WIDTH ** -0.5),
        "dw_b": nrm(ks[12], (L, CONV_CH), 0.02),
        "conv_ln_g": gain(ks[13], (L, CONV_CH)),
        "conv_ln_b": nrm(ks[14], (L, CONV_CH), 0.02),
        "conv_proj": nrm(ks[15], (L, CONV_CH, D_MODEL), CONV_CH ** -0.5),
        "w_out": nrm(ks[16], (L, D_MODEL, D_MODEL), D_MODEL ** -0.5),
        "ffn2_norm": gain(ks[17], (L, D_MODEL)),
        "ffn2_wgu": nrm(ks[18], (L, D_MODEL, 2 * D_FF), D_MODEL ** -0.5),
        "ffn2_wdown": nrm(ks[19], (L, D_FF, D_MODEL), D_FF ** -0.5),
        "ple_proj": nrm(ks[20], (L, PLE_DIM, D_MODEL), PLE_DIM ** -0.5),
        "ple_norm": gain(ks[21], (L, D_MODEL)),
        "ple_gate_norm": gain(ks[22], (L, D_MODEL)),
        "ple_gate_w": nrm(ks[23], (L, D_MODEL, D_MODEL), D_MODEL ** -0.5),
    }

def first_block(x, p, ffn1_norm, ffn1_wgu, ffn1_wdown, mix_norm, w_in, q_norm, k_norm, sinks,
              attn_proj, dw_w, dw_b, conv_ln_g, conv_ln_b, conv_proj, w_out,
              ffn2_norm, ffn2_wgu, ffn2_wdown, ple_proj, ple_norm, ple_gate_norm, ple_gate_w):
    B, S = x.shape[0], x.shape[1]
    cos, sin = rope_tables(S)
    offs = np.cumsum((0,) + SPLIT_SIZES)
    for i in range(DEPTH):
        x = x + 0.5 * swiglu(rmsnorm(x, ffn1_norm[i]), ffn1_wgu[i], ffn1_wdown[i])

        h = rmsnorm(x, mix_norm[i])
        z = h @ w_in[i]
        zq, zk, zv, zc, zg = [z[..., offs[j]:offs[j + 1]] for j in range(len(SPLIT_SIZES))]

        q = rmsnorm(zq.reshape(B, S, N_Q_HEADS, HEAD_DIM), q_norm[i])
        k = rmsnorm(zk.reshape(B, S, N_KV_HEADS, HEAD_DIM), k_norm[i])
        v = zv.reshape(B, S, N_KV_HEADS, HEAD_DIM)
        q = partial_rope(q, cos, sin)
        k = partial_rope(k, cos, sin)
        a = sliding_window_attention(q, k, v, sinks[i]) @ attn_proj[i]

        ca, cb = jnp.split(zc, 2, axis=-1)
        u = ca * jax.nn.sigmoid(cb)
        u = causal_depthwise_conv(u, dw_w[i], dw_b[i])
        c = jax.nn.silu(layernorm(u, conv_ln_g[i], conv_ln_b[i])) @ conv_proj[i]

        ga, gb = jnp.split(zg, 2, axis=-1)
        merged = jax.nn.sigmoid(ga) * a + jax.nn.sigmoid(gb) * c
        x = x + merged @ w_out[i]

        x = x + 0.5 * swiglu(rmsnorm(x, ffn2_norm[i]), ffn2_wgu[i], ffn2_wdown[i])

        e = rmsnorm(p[i] @ ple_proj[i], ple_norm[i])
        gate = jax.nn.sigmoid(rmsnorm(x, ple_gate_norm[i]) @ ple_gate_w[i])
        x = x + gate * e
    return x


N_MOD = 9
GLA_HEADS = 4
GLA_DK = D_MODEL // 2
GLA_DV = D_MODEL
GLA_HK = GLA_DK // GLA_HEADS
GLA_HV = GLA_DV // GLA_HEADS
GLA_RANK = 16
GLA_TAU = 16.0
GLA_CHUNK = 64
FOX_HEADS = 16
FOX_HD = D_MODEL // FOX_HEADS
FOX_W = FOX_HEADS * FOX_HD
Q_BLOCK = 128
SPLITS = (GLA_DK, GLA_DK, GLA_DV, GLA_RANK, GLA_DV, FOX_W, FOX_W, FOX_W, FOX_HEADS, D_MODEL, D_MODEL)
IN_COLS = 2 * GLA_DK + 2 * GLA_DV + GLA_RANK + 3 * FOX_W + FOX_HEADS + 2 * D_MODEL


def rmsnorm_2(x, g):
    xf = x.astype(jnp.float32)
    y = xf * lax.rsqrt(jnp.mean(xf * xf, axis=-1, keepdims=True) + EPS)
    return (y * g.astype(jnp.float32)).astype(x.dtype)

def swiglu_2(h, w_gu, w_dn):
    g, u = jnp.split(h @ w_gu, 2, axis=-1)
    return (jax.nn.silu(g) * u) @ w_dn

def gla_chunked(q, k, v, log_a):
    B, H, T, dk = q.shape
    dv = v.shape[-1]
    C = GLA_CHUNK
    N = T // C

    def to_chunks(a):
        return a.reshape(B, H, N, C, a.shape[-1]).transpose(2, 0, 1, 3, 4)

    qc, kc, vc, gc = to_chunks(q), to_chunks(k), to_chunks(v), to_chunks(log_a)
    causal = jnp.tril(jnp.ones((C, C), dtype=bool))[:, :, None]

    def step(S, inp):
        qi, ki, vi, gi = inp
        b = jnp.cumsum(gi, axis=2)
        o_inter = jnp.einsum('bhtd,bhde->bhte', qi * jnp.exp(b), S)
        diff = b[:, :, :, None, :] - b[:, :, None, :, :]
        decay = jnp.exp(jnp.where(causal, diff, -jnp.inf))
        A = jnp.einsum('bhtd,bhsd,bhtsd->bhts', qi, ki, decay)
        o = o_inter + jnp.einsum('bhts,bhse->bhte', A, vi)
        b_last = b[:, :, -1:, :]
        S_new = jnp.exp(b_last[:, :, 0, :, None]) * S + jnp.einsum(
            'bhsd,bhse->bhde', ki * jnp.exp(b_last - b), vi)
        return S_new, o

    S0 = jnp.zeros((B, H, dk, dv), jnp.float32)
    _, o = lax.scan(step, S0, (qc, kc, vc, gc))
    return o.transpose(1, 2, 0, 3, 4).reshape(B, H, T, dv)

def fox_attention(q, k, v, logf):
    B, H, T, hd = q.shape
    F = jnp.cumsum(logf, axis=-1)
    nb = T // Q_BLOCK
    qb = q.reshape(B, H, nb, Q_BLOCK, hd).transpose(2, 0, 1, 3, 4)
    Fb = F.reshape(B, H, nb, Q_BLOCK).transpose(2, 0, 1, 3)
    kpos = jnp.arange(T)
    scale = hd ** -0.5

    def block(args):
        qi, Fi, i = args
        s = jnp.einsum('bhqd,bhkd->bhqk', qi, k).astype(jnp.float32) * scale
        s = s + Fi[..., None] - F[:, :, None, :]
        qpos = i * Q_BLOCK + jnp.arange(Q_BLOCK)
        s = jnp.where(kpos[None, :] <= qpos[:, None], s, -jnp.inf)
        p = jax.nn.softmax(s, axis=-1)
        return jnp.einsum('bhqk,bhkd->bhqd', p.astype(v.dtype), v)

    o = lax.map(block, (qb, Fb, jnp.arange(nb)))
    return o.transpose(1, 2, 0, 3, 4).reshape(B, H, T, hd)

def token_mixer(h, w_in, w_a2, b_a, b_f, g_gla, w_pa, w_pb, w_out):
    B, T, _ = h.shape
    f32 = jnp.float32
    z = h @ w_in
    cuts = np.cumsum(SPLITS)[:-1].tolist()
    q_a, k_a, v_a, a_low, r_a, q_b, k_b, v_b, f_b, gate_a, gate_b = jnp.split(z, cuts, axis=-1)

    def heads(t, n):
        return t.reshape(B, T, n, -1).transpose(0, 2, 1, 3)

    log_a = jax.nn.log_sigmoid((a_low @ w_a2 + b_a).astype(f32)) / GLA_TAU
    o_a = gla_chunked(heads(q_a.astype(f32) * (GLA_HK ** -0.5), GLA_HEADS),
                      heads(k_a.astype(f32), GLA_HEADS),
                      heads(v_a.astype(f32), GLA_HEADS),
                      heads(log_a, GLA_HEADS))
    o_a = rmsnorm_2(o_a.transpose(0, 2, 1, 3), g_gla.reshape(GLA_HEADS, GLA_HV))
    o_a = o_a.astype(h.dtype).reshape(B, T, GLA_DV) * jax.nn.silu(r_a)

    logf = jax.nn.log_sigmoid((f_b + b_f).astype(f32)).transpose(0, 2, 1)
    o_b = fox_attention(heads(q_b, FOX_HEADS), heads(k_b, FOX_HEADS), heads(v_b, FOX_HEADS), logf)
    o_b = o_b.transpose(0, 2, 1, 3).reshape(B, T, FOX_W)

    merged = jax.nn.sigmoid(gate_a) * (o_a @ w_pa) + jax.nn.sigmoid(gate_b) * (o_b @ w_pb)
    return merged @ w_out

def second_inputs(seed: int = 0) -> dict:
    key = jax.random.key(seed)
    ks = jax.random.split(key, 20)
    L, D = DEPTH, D_MODEL
    nrm = jax.random.normal

    def w(k, shape, fan_in):
        return nrm(k, shape, jnp.float32) * fan_in ** -0.5

    return {
        "x": nrm(ks[0], (BATCH, SEQ, D), jnp.float32),
        "c": nrm(ks[1], (BATCH, D), jnp.float32),
        "w_ada": w(ks[2], (L, D, N_MOD * D), D) * 0.5,
        "b_ada": 0.02 * nrm(ks[3], (L, N_MOD * D), jnp.float32),
        "g_pre": 1.0 + 0.05 * nrm(ks[4], (L, 3, D), jnp.float32),
        "g_post": 1.0 + 0.05 * nrm(ks[5], (L, 3, D), jnp.float32),
        "w_gu1": w(ks[6], (L, D, 2 * D_FF), D),
        "w_dn1": w(ks[7], (L, D_FF, D), D_FF),
        "w_gu2": w(ks[8], (L, D, 2 * D_FF), D),
        "w_dn2": w(ks[9], (L, D_FF, D), D_FF),
        "w_in": w(ks[10], (L, D, IN_COLS), D),
        "w_a2": w(ks[11], (L, GLA_RANK, GLA_DK), GLA_RANK),
        "b_a": 0.1 * nrm(ks[12], (L, GLA_DK), jnp.float32),
        "b_f": 1.0 + 0.1 * nrm(ks[13], (L, FOX_HEADS), jnp.float32),
        "g_gla": 1.0 + 0.05 * nrm(ks[14], (L, GLA_DV), jnp.float32),
        "w_pa": w(ks[15], (L, GLA_DV, D), GLA_DV),
        "w_pb": w(ks[16], (L, FOX_W, D), FOX_W),
        "w_out": w(ks[17], (L, D, D), D),
    }

def second_block(x, c, w_ada, b_ada, g_pre, g_post, w_gu1, w_dn1, w_gu2, w_dn2,
              w_in, w_a2, b_a, b_f, g_gla, w_pa, w_pb, w_out):
    B = x.shape[0]
    for l in range(DEPTH):
        mods = (jax.nn.silu(c) @ w_ada[l] + b_ada[l]).reshape(B, N_MOD, 1, D_MODEL)
        sh1, sc1, gt1, sh2, sc2, gt2, sh3, sc3, gt3 = [mods[:, i] for i in range(N_MOD)]

        h = rmsnorm_2(x, g_pre[l, 0]) * (1 + sc1) + sh1
        x = x + 0.5 * gt1 * rmsnorm_2(swiglu_2(h, w_gu1[l], w_dn1[l]), g_post[l, 0])

        h = rmsnorm_2(x, g_pre[l, 1]) * (1 + sc2) + sh2
        y = token_mixer(h, w_in[l], w_a2[l], b_a[l], b_f[l], g_gla[l], w_pa[l], w_pb[l], w_out[l])
        x = x + gt2 * rmsnorm_2(y, g_post[l, 1])

        h = rmsnorm_2(x, g_pre[l, 2]) * (1 + sc3) + sh3
        x = x + 0.5 * gt3 * rmsnorm_2(swiglu_2(h, w_gu2[l], w_dn2[l]), g_post[l, 2])
    return x


def setup_inputs(seed=0):
    out = dict(first_inputs(seed))
    for name, value in second_inputs(seed + 1).items():
        if name != "x":
            out[name + "_2"] = value
    return out


def reference(
    x, p, ffn1_norm, ffn1_wgu, ffn1_wdown, mix_norm, w_in, q_norm, k_norm, sinks, attn_proj,
    dw_w, dw_b, conv_ln_g, conv_ln_b, conv_proj, w_out, ffn2_norm, ffn2_wgu, ffn2_wdown,
    ple_proj, ple_norm, ple_gate_norm, ple_gate_w, c_2, w_ada_2, b_ada_2, g_pre_2, g_post_2,
    w_gu1_2, w_dn1_2, w_gu2_2, w_dn2_2, w_in_2, w_a2_2, b_a_2, b_f_2, g_gla_2, w_pa_2, w_pb_2,
    w_out_2,
):
    x = first_block(
        x, p, ffn1_norm, ffn1_wgu, ffn1_wdown, mix_norm, w_in, q_norm, k_norm, sinks, attn_proj,
        dw_w, dw_b, conv_ln_g, conv_ln_b, conv_proj, w_out, ffn2_norm, ffn2_wgu, ffn2_wdown,
        ple_proj, ple_norm, ple_gate_norm, ple_gate_w,
    )
    return second_block(
        x, c_2, w_ada_2, b_ada_2, g_pre_2, g_post_2, w_gu1_2, w_dn1_2, w_gu2_2, w_dn2_2, w_in_2,
        w_a2_2, b_a_2, b_f_2, g_gla_2, w_pa_2, w_pb_2, w_out_2,
    )


_drawn_inputs = setup_inputs


def setup_inputs(seed=0):
    import zlib

    import numpy as np

    out = dict(_drawn_inputs(seed))
    spreads = {}
    factors = {'mix_norm': 2.753,
     'q_norm': 8.0,
     'k_norm': 8.0,
     'sinks': 32.934,
     'dw_b': 4.133,
     'conv_ln_g': 3.019,
     'conv_ln_b': 8.0,
     'ffn2_norm': 3.12,
     'ple_gate_norm': 42.515,
     'g_post_2': 12.546,
     'b_a_2': 6.257,
     'b_f_2': 64.0,
     'g_gla_2': 29.6,
     'ple_norm': 6.191,
     'w_pb_2': 4.959}
    for name, (base, spread) in spreads.items():
        noise = np.random.default_rng([zlib.crc32(name.encode()), seed]).standard_normal(out[name].shape)
        drawn = base * np.exp(spread * noise) if base else spread * noise
        out[name] = __import__('jax').numpy.asarray(drawn.astype(out[name].dtype))
    for name, factor in factors.items():
        out[name] = (out[name] * factor).astype(out[name].dtype)
    return out
```

```python
from contextlib import ExitStack

import concourse.bass as bass
from concourse import mybir

F32 = mybir.dt.float32
F32R = mybir.dt.float32r
BF16 = mybir.dt.bfloat16
I32 = mybir.dt.int32
ALU = mybir.AluOpType
ACT = mybir.ActivationFunctionType
AX = mybir.AxisListType.X

P = 128
S = 256
T = S // P
D = 1024
KC = D // P
FF = 2816
FC = FF // P
HALF = 256
UPB = FF // HALF
UNIT = 1024
RAW = 8
SPLIT = 4
EPS = 1e-6
NEG = -1e30
TAPS = 31
NH = 16
HD = 64
GH = 4
GDK = 128
GDV = 256
LEVELS = [64, 32, 16, 8, 4, 2, 1]
AUG = HD + 2

ROWS = ([("dw_w", i) for i in range(TAPS)] + [("dw_b", 0), ("conv_ln_g", 0), ("conv_ln_b", 0), ("ffn1_norm", 0),
        ("mix_norm", 0), ("ffn2_norm", 0), ("ple_gate_norm", 0), ("g_pre_2", 0), ("g_pre_2", 1), ("g_pre_2", 2),
        ("c_2", 0)])
ROW = {}
for _i, (_n, _k) in enumerate(ROWS):
    ROW[(_n, _k)] = _i
NROW = len(ROWS)

C_ID, C_ONES, C_TRI, C_D, C_W, C_COS, C_SIN, C_GLA = 0, 128, 256, 384, 512, 640, 656, 672
NGLA = 1 + len(LEVELS)
NCONST = C_GLA + NGLA * P


def shape_constants():
    import numpy as np

    t = np.zeros((P, NCONST), np.float32)
    i = np.arange(P)
    t[:, C_ID:C_ID + P] = np.eye(P)
    t[:, C_ONES:C_ONES + P] = 1.0
    t[:, C_TRI:C_TRI + P] = i[:, None] <= i[None, :]
    t[:, C_D:C_D + P] = np.where(i[None, :] <= i[:, None], 0.0, NEG)
    t[:, C_W:C_W + P] = np.where(i[None, :] > i[:, None], 0.0, NEG)
    inv = np.float32(500000.0) ** (-np.arange(0, 16, 2, dtype=np.float32) / np.float32(16))
    ang = np.arange(S, dtype=np.float32)[:, None] * inv[None, :].astype(np.float32)
    for n in range(T):
        t[:, C_COS + 8 * n:C_COS + 8 * n + 8] = np.cos(ang[n * P:(n + 1) * P])
        t[:, C_SIN + 8 * n:C_SIN + 8 * n + 8] = np.sin(ang[n * P:(n + 1) * P])
    s, q = i[:, None], i[None, :]
    t[:, C_GLA:C_GLA + P] = s == q
    for n, L in enumerate(LEVELS):
        pair = (s // (2 * L) == q // (2 * L)) & (s // L % 2 == 0) & (q // L % 2 == 1)
        t[:, C_GLA + (n + 1) * P:C_GLA + (n + 2) * P] = pair
    return t


def two_blocks(nc, A, consts, out):
    ctx = ExitStack()
    with ctx:
        at = [nc.sbuf_base + 31 & ~31]

        def place(name, shape, dt=F32, base=None):
            size = 1
            for n in shape[1:]:
                size *= n
            size *= 2 if dt == BF16 else 4
            if base is None:
                base = at[0]
                at[0] += size + 31 & ~31
            return nc.alloc_sbuf_tensor_at(name, shape, dt, offset=base), base, base + (size + 31 & ~31)

        def keep(name, shape, dt=F32):
            return place(name, shape, dt)[0]

        raw = keep("raw", [P, RAW, UNIT])
        w_hi = keep("w_hi", [P, SPLIT, UNIT], F32R)
        w_lo = keep("w_lo", [P, SPLIT, UNIT], F32R)
        x = keep("x", [P, T, D])
        a_hi = keep("a_hi", [P, KC, S], F32R)
        a_lo = keep("a_lo", [P, KC, S], F32R)
        b_hi, B0, _ = place("b_hi", [P, KC, S], F32R)
        b_lo = keep("b_lo", [P, KC, S], F32R)
        GT, GT0, _ = place("GT", [P, 3, D])
        const = keep("const", [P, C_GLA])
        identb = keep("identb", [P, P], BF16)
        maskD = keep("maskD", [P, P], BF16)
        maskWD = keep("maskWD", [P, 2 * P], BF16)
        par = keep("par", [P, KC, NROW])
        csil = keep("csil", [P, KC])
        modA = keep("modA", [P, 3, KC])
        modB = keep("modB", [P, 3, KC])
        gq = keep("gq", [P, HD])
        gk = keep("gk", [P, HD])
        sinkb = keep("sinkb", [P, NH])
        bfb = keep("bfb", [P, NH])
        baT = keep("baT", [P, GH])
        wa2 = keep("wa2", [16, 512])
        ss = keep("ss", [P, 2])
        rstd = keep("rstd", [P, 2])
        pss = keep("pss", [P, 2])
        prs = keep("prs", [P, 2])
        rt = keep("rt", [P, 3, 18])
        rs18 = keep("rs18", [P, 18])
        b_lo_f = keep("b_lo_f", [P, 2 * S])
        st = keep("st", [P, 2, 6, 4])
        ARENA2 = at[0]
        ada = keep("ada", [P, 3, D])
        acc_m = keep("acc_m", [P, 2, D])
        ada_t = keep("ada_t", [P, D])
        brow = keep("brow", [1, D])
        ARENA = at[0]
        hid_hi, _, e = place("hid_hi", [P, FC, S], F32R, ARENA)
        hid_lo, _, e = place("hid_lo", [P, FC, S], F32R, e)
        HB = e
        h, _, _ = place("h", [P, T, D], F32, HB)
        sg, _, e = place("sg", [P, 2, T, HALF], F32, HB)
        hid, _, END = place("hid", [P, 2, T, HALF], F32, e)
        assert END <= nc.sbuf_usable_end, (END, nc.sbuf_usable_end)
        prow, _, _ = place("prow", [NROW, D], F32, ARENA)
        csg, _, e = place("csg", [P, 2, T, HALF], F32, ARENA)
        cub, _, e = place("cub", [P, 2, T, HALF], F32, e)
        uT, _, e = place("uT", [P, KC, S + TAPS - 1], F32, e)
        y, _, e = place("y", [P, KC, S], F32, e)
        qkv, Q0, e = place("qkv", [P, T, 1280], F32, e)
        gates, _, e = place("gates", [P, T, 2 * D], F32, e)
        assert e <= END, (e, END)
        qT, _, _ = place("qT", [P, KC, S], F32, ARENA)
        cf, _, _ = place("cf", [P, KC, S], F32, ARENA)
        ysq, _, e = place("ysq", [P, KC, S], F32, Q0)
        lnb, _, e = place("lnb", [P, 2, S], F32, e)
        lnt, _, _ = place("lnt", [P, 3, S], F32, B0)
        qsq, _, e = place("qsq", [P, 18 * HD], F32, B0)
        rope, _, e = place("rope", [P, 4, 18, 8], F32, e)
        pr, _, e = place("pr", [P, 2, 512], F32, B0)
        pt, _, e = place("pt", [P, 2, 512], F32, e)
        kTz, _, e = place("kTz", [P, 2, 2, S], F32, e)
        kdup, _, e = place("kdup", [P, T, 2, 2, HD], F32, e)
        assert e <= GT0
        emb, _, e = place("emb", [P, T, D], F32, ARENA)
        grow, _, e = place("grow", [P, D], F32, e)
        pin, _, e = place("pin", [P, T, 256], F32, e)
        assert e <= HB
        va, _, e = place("va", [P, T, D], F32, ARENA2)
        ra, _, e = place("ra", [P, T, D], F32, e)
        gates2, _, _ = place("gates2", [P, T, 2 * D], F32, ARENA2)
        qa, QA0, e = place("qa", [P, GH, S], F32, e)
        ka, _, e = place("ka", [P, GH, S], F32, e)
        ggla, _, e = place("ggla", [P, D], F32, e)
        bc, _, e = place("bc", [P, GH, S], F32, e)
        AT, _, e = place("AT", [P, 3, GH, P], F32, e)
        qb, _, e = place("qb", [AUG, NH, S], F32, e)
        kb, _, e = place("kb", [AUG, NH, S], F32, e)
        vb, _, e = place("vb", [P, T, D], F32, e)
        sm, _, e = place("sm", [P, T, 32], F32, e)
        lf, _, e = place("lf", [P, 3, T, NH], F32, e)
        Fc, _, e = place("Fc", [P, T, NH], F32, e)
        alT, _, e = place("alT", [16, S], F32, e)
        ga_ss, _, e = place("ga_ss", [P, 5, 8], F32, e)
        assert e <= END, (e, END)
        glam, _, _ = place("glam", [P, NGLA, P], F32, GT0)
        zt, _, _ = place("zt", [P, T, 512], F32, B0)
        aug, _, e = place("aug", [P, T, 8, AUG], F32, B0)
        ya, _, e = place("ya", [P, GH, S], F32, e)
        la, _, e = place("la", [P, GH, S], F32, e)
        assert e <= GT0
        dd, _, e = place("dd", [P, 2, 512], F32, B0)
        gtmp, _, e = place("gtmp", [P, 512], F32, e)
        qd, _, e = place("qd", [P, GH * S], F32, e)
        kd, _, e = place("kd", [P, GH * S], F32, e)
        assert e <= GT0
        pr2, _, e = place("pr2", [P, 2, 512], F32, QA0)
        pt2, _, e = place("pt2", [P, 2, 512], F32, e)

        ps = ctx.enter_context(nc.psum_tensor("ps", [P, 8, 512], F32))

        def acc(t, s):
            return ps[:, 2 * t + s, :]

        def wide(t):
            return ps[:, 2 * t:2 * t + 2, :].rearrange("p b n -> p (b n)")

        ident = const[:, C_ID:C_ID + P]
        ones = const[:, C_ONES:C_ONES + P]

        sems = {}

        def sem(name):
            if name not in sems:
                sems[name] = ctx.enter_context(nc.semaphore(name))
            return sems[name]

        units = []

        def cols_units(W, c0, n, c1=None):
            v = W.rearrange("(c p) n -> p c n", p=P)
            first = len(units)
            for i in range(0, KC, 2):
                if c1 is None:
                    units.append(([v[:, i:i + 2, c0:c0 + n]], 2, n))
                else:
                    units.append(([v[:, i:i + 2, c0:c0 + n // 2], v[:, i:i + 2, c1:c1 + n // 2]], 2, n))
            return first

        def row_units(W):
            v = W.rearrange("(c p) n -> p c n", p=P)
            first = len(units)
            for i in range(W.shape[0] // P):
                units.append(([v[:, i:i + 1, :]], 1, D))
            return first

        def ffn_units(wgu, wdn):
            up = [cols_units(wgu, j * HALF, 2 * HALF, FF + j * HALF) for j in range(UPB)]
            return up[0], row_units(wdn)

        ffn = [None] * 4
        ffn[0] = ffn_units(A["ffn1_wgu"][0], A["ffn1_wdown"][0])
        w_in = A["w_in"][0]
        CA, CB, ZG = 1280, 2304, 3328
        u_mix = [cols_units(w_in, CA + j * HALF, 512, CB + j * HALF) for j in range(4)]
        u_mix += [cols_units(w_in, 0, 512), cols_units(w_in, 512, 512), cols_units(w_in, 1024, 256)]
        u_mix += [cols_units(w_in, ZG + 512 * i, 512) for i in range(4)]
        u_ap = row_units(A["attn_proj"][0])
        u_cp = row_units(A["conv_proj"][0])
        u_wo = row_units(A["w_out"][0])
        ffn[1] = ffn_units(A["ffn2_wgu"][0], A["ffn2_wdown"][0])
        u_pp = row_units(A["ple_proj"][0])
        u_pg = row_units(A["ple_gate_w"][0])
        ffn[2] = ffn_units(A["w_gu1_2"][0], A["w_dn1_2"][0])
        w_in2 = A["w_in_2"][0]
        M2 = len(units)
        v = w_in2.rearrange("(c p) n -> p c n", p=P)
        units.append(([v[:, :, 2048:2064], v[:, :, 6160:6176]], KC, 32))
        c2 = [0, 512, 1024, 1536, 2064, 2576, 3088, 3600, 4112, 4624, 5136, 5648, 6176, 6688, 7200, 7712]
        u_mix2 = [M2] + [cols_units(w_in2, c, 512) for c in c2]
        u_pa = row_units(A["w_pa_2"][0])
        u_pb = row_units(A["w_pb_2"][0])
        u_wo2 = row_units(A["w_out_2"][0])
        ffn[3] = ffn_units(A["w_gu2_2"][0], A["w_dn2_2"][0])
        NU = len(units)

        count = [0] * RAW
        need = []
        for u in range(NU):
            count[u % RAW] += 16 * len(units[u][0])
            need.append(count[u % RAW])

        landed = [sem(f"raw_landed{r}") for r in range(RAW)]
        hi_ready, lo_ready, used = sem("w_hi_ready"), sem("w_lo_ready"), sem("unit_used")

        class Stream:

            def __init__(self, part):
                self.part, self.at = part, 0

            def to(self, n):
                while self.at < min(n, NU):
                    self.part(self.at)
                    self.at += 1

        NORM = {"f0": 0, "mix": 1, "f1": 2, "gate": 3, "f2": 4, "mix2": 5, "f3": 6}
        TURN = {"f0": 0, "mix": 1, "merge": 2, "f1": 3, "gate": 4, "f2": 5, "mix2": 6, "oa": 7, "merge2": 8, "f3": 9}
        SCALE_ROW = {"f0": ("ffn1_norm", 0), "mix": ("mix_norm", 0), "f1": ("ffn2_norm", 0), "gate": ("ple_gate_norm", 0)}
        MODS = {"f2": 0, "mix2": 1, "f3": 2}
        FFN = ["f0", "f1", "f2", "f3"]
        POST = {"emb": 0, "f2": 1, "mix2": 2, "f3": 3}

        CONV_IN_MIX = 24 * 6
        MOD_AT = {("f0", UPB): (0,), ("mix", 6): (1,), ("mix", 8): (2,), ("mix", 10): (3,), ("f1", 1): (4,), ("f1", 3): (5,),
                  ("f1", 6): (6,), ("f1", 9): (7,), ("f1", UPB): (8,)}
        NSTEP = 2 + len(LEVELS)

        block = ctx.enter_context(nc.Block())

        GROUPS = [(0, 4 * i, 4, 1) for i in range(4)] + [(1, 2 * i, 2, 2) for i in range(8)]
        NG = len(GROUPS)

        def exps(m, i):
            n = (NG + sum(g[2] for g in GROUPS)) * m
            return n + sum(g[2] + (m == 0) for g in GROUPS[:i + 1])

        ENDS = {1: (0, 0), 3: (0, 1), 7: (1, 0), 11: (1, 1)}

        @block.sync
        def _(sp):
            def row(name, k):
                a = A[name]
                if name in ("dw_w", "g_pre_2"):
                    return a[0, k:k + 1, :]
                return a[0:1, :]

            def load_unit(u):
                src, nk, n = units[u]
                if u >= RAW:
                    sp.wait_ge(lo_ready, u - RAW + 1)
                dst = raw[:, u % RAW, 0:nk * n].rearrange("p (c n) -> p c n", c=nk)
                if len(src) == 1:
                    sp.dma_start(dst, src[0]).then_inc(landed[u % RAW], 16)
                else:
                    sp.dma_start(dst[:, :, 0:n // 2], src[0]).then_inc(landed[u % RAW], 16)
                    sp.dma_start(dst[:, :, n // 2:n], src[1]).then_inc(landed[u % RAW], 16)

            sp.dma_start(x[:, :, :], A["x"][0].rearrange("(t p) d -> p t d", p=P)).then_inc(sem("x_landed"), 16)
            sp.dma_start(const[:, :], consts[:, 0:C_GLA]).then_inc(sem("const_landed"), 16)
            sp.dma_start(prow[0:TAPS, :], A["dw_w"][0]).then_inc(sem("prow_landed"), 16)
            for i, (n, k) in enumerate(ROWS):
                if n != "dw_w":
                    sp.dma_start(prow[i:i + 1, :], row(n, k)).then_inc(sem("prow_landed"), 16)
            for u in range(4):
                load_unit(u)
            for n, (dst, src) in enumerate([
                (gq[:, :], A["q_norm"]), (gk[:, :], A["k_norm"]), (sinkb[:, :], A["sinks"]), (bfb[:, :], A["b_f_2"]),
            ]):
                sp.dma_start(dst, src[0].partition_broadcast(P)).then_inc(sem("small_landed"), 16)
            sp.dma_start(baT[:, :], A["b_a_2"][0].rearrange("(h p) -> p h", p=P), allow_slow_non_contiguous=True).then_inc(sem("small_landed"), 16)
            sp.dma_start(wa2[:, :], A["w_a2_2"][0]).then_inc(sem("small_landed"), 16)
            for u in range(4, u_pp):
                load_unit(u)
            sp.wait_ge(used, u_pp)
            sp.dma_start(pin[:, :, :], A["p"][0, 0].rearrange("(t p) d -> p t d", p=P)).then_inc(sem("pin_landed"), 16)
            sp.dma_start(grow[:, :], A["ple_norm"][0].partition_broadcast(P)).then_inc(sem("grow_landed"), 16)
            for u in range(u_pp, M2 + 4):
                load_unit(u)
            sp.wait_ge(sem("x_ready"), 10)
            sp.dma_start(glam[:, :, :], consts[:, C_GLA:NCONST].rearrange("p (m n) -> p m n", n=P)).then_inc(sem("glam_landed"), 16)
            sp.dma_start(ggla[:, :], A["g_gla_2"][0].partition_broadcast(P)).then_inc(sem("glam_landed"), 16)
            for u in range(M2 + 4, NU):
                load_unit(u)
            for t in range(T):
                sp.wait_ge(sem("x_ready"), 13 + t)
                sp.dma_start(out[0, t * P:(t + 1) * P, :], x[:, t, :]).then_inc(sem("out_stored"), 16)
            sp.wait_ge(sem("out_stored"), 16 * T)

        @block.gpsimd
        def _(pool):
            link = [0]

            def then(ins):
                link[0] += 1
                ins.then_inc(sem("pool_step"), 1)
                pool.wait_ge(sem("pool_step"), link[0])

            w_ada = A["w_ada_2"][0].rearrange("(c p) n -> c p n", p=P)

            def load(i):
                m, k = i // KC, i % KC
                pool.dma_start(ada[:, i % 3, :], w_ada[k, :, m * D:(m + 1) * D]).then_inc(sem(f"ada_landed{i % 3}"), 16)

            for g in range(3):
                pool.dma_start(GT[:, g, :], A["g_post_2"][0, g].partition_broadcast(P)).then_inc(sem("gpost_landed"), 16)
            for i in range(3):
                load(i)
            pool.wait_ge(sem("csil_ready"), 1)
            for m in range(9):
                pool.dma_start(brow[:, :], A["b_ada_2"][0:1, m * D:(m + 1) * D]).then_inc(sem("brow_landed"), 16)
                if m >= 2:
                    pool.wait_ge(sem("mod_summed"), m - 1)
                for k in range(KC):
                    i = m * KC + k
                    pool.wait_ge(sem(f"ada_landed{i % 3}"), 16 * (i // 3 + 1))
                    if k == 0:
                        then(pool.tensor_scalar(acc_m[:, m % 2, :], ada[:, i % 3, :], csil[:, 0:1], None, ALU.mult))
                    else:
                        then(pool.tensor_scalar(ada_t[:, :], ada[:, i % 3, :], csil[:, k:k + 1], None, ALU.mult))
                        then(pool.tensor_tensor(acc_m[:, m % 2, :], acc_m[:, m % 2, :], ada_t[:, :], ALU.add))
                    if i + 3 < 9 * KC:
                        load(i + 3)
                pool.wait_ge(sem("brow_landed"), 16 * (m + 1))
                pool.tensor_tensor(acc_m[0:1, m % 2, :], acc_m[0:1, m % 2, :], brow[:, :], ALU.add).then_inc(sem("mod_ready"), 1)
                pool.wait_ge(sem("mod_ready"), m + 1)

        @block.scalar
        def _(act):
            def hi_part(u):
                _, nk, n = units[u]
                act.wait_ge(landed[u % RAW], need[u])
                if u >= SPLIT:
                    act.wait_ge(used, u - SPLIT + 1)
                act.activation(w_hi[:, u % SPLIT, 0:nk * n], raw[:, u % RAW, 0:nk * n], ACT.Copy).then_inc(hi_ready, 1)

            w = Stream(hi_part)

            def norm_squares(key, junk):
                q = NORM[key]
                for t in range(T):
                    if q == 0:
                        act.wait_ge(sem("x_landed"), 16)
                    else:
                        act.wait_ge(sem("x_ready"), 2 * q - 1 + t)
                    if TURN[key] > 0:
                        act.wait_ge(sem("turned"), 4 * TURN[key])
                    act.activation(junk[:, t, :], x[:, t, :], ACT.Square, accum_out=ss[:, t:t + 1]).then_inc(sem("ss_ready"), 1)

            def turned_hi(key, hi=a_hi):
                k = TURN[key]
                for c in range(KC):
                    if c % 2 == 0:
                        act.wait_ge(sem("turned"), 4 * k + c // 2 + 1)
                    src = ps[:, 4 + c // 2, (c % 2) * S:(c % 2 + 1) * S]
                    if key in SCALE_ROW:
                        r = ROW[SCALE_ROW[key]]
                        i = act.activation(hi[:, c, :], src, ACT.Copy, scale=par[:, c, r:r + 1])
                    elif key in MODS:
                        g = MODS[key]
                        i = act.activation(hi[:, c, :], src, ACT.Identity, scale=modA[:, g, c:c + 1], bias=modB[:, g, c:c + 1])
                    else:
                        i = act.activation(hi[:, c, :], src, ACT.Copy)
                    i.then_inc(sem("act_hi"), 1)

            def post_squares(key, junk):
                for t in range(T):
                    act.activation(junk[:, t, :], wide(t), ACT.Square, accum_out=pss[:, t:t + 1]).then_inc(sem("pss_ready"), 1)

            def ffn_part(f):
                up, dn = ffn[f]
                for j in range(UPB):
                    w.to(up + 4 * j + 6)
                    if j >= 1:
                        hidden_hi(f, j - 1)
                    w.to(up + 4 * j + 8)
                    act.wait_ge(used, up + 4 * j + 4)
                    for t in range(T):
                        if j >= 2:
                            act.wait_ge(sem("hid_ready"), f * UPB + j - 1)
                        act.activation(sg[:, j % 2, t, :], acc(t, j % 2)[:, 0:HALF], ACT.Silu).then_inc(sem("silu_ready"), 1)
                hidden_hi(f, UPB - 1)
                w.to(dn + FC + 4)

            def hidden_hi(f, j):
                act.wait_ge(sem("hid_turned"), f * UPB + j + 1)
                act.activation(hid_hi[:, 2 * j:2 * j + 2, :].rearrange("p c n -> p (c n)"), ps[:, 4 + j % 2, :], ACT.Copy)\
                   .then_inc(sem("hid_hi_ready"), 1)

            def attention_part(m):
                prb, ptb = (pr, pt) if m == 0 else (pr2, pt2)
                g0, e0 = NG * m, 4 * m
                for i in range(NG + 3):
                    if i < NG:
                        n, h0, nh, nk = GROUPS[i]
                        act.wait_ge(sem("bias_ready"), g0 + i + 1)
                        if i >= 2:
                            act.wait_ge(sem("probs_turned"), g0 + i - 1)
                        L = nk * P
                        for q in range(nh):
                            act.activation(prb[:, i % 2, q * L:(q + 1) * L], ps[:, 4 + i % 4, q * L:(q + 1) * L], ACT.Exp,
                                           bias=st[:, i % 2, 1, q:q + 1], scale=HD ** -0.5 if m == 0 else 1.0,
                                           accum_out=st[:, i % 2, 2, q:q + 1]).then_inc(sem("exp_done"), 1)
                        if m == 0:
                            act.activation(st[:, i % 2, 3, 0:nh], st[:, i % 2, 4, 0:nh], ACT.Exp).then_inc(sem("exp_done"), 1)
                    if 2 <= i < NG + 2:
                        act.wait_ge(sem("probs_turned"), g0 + i - 1)
                        if i >= 4:
                            act.wait_ge(sem("values_done"), g0 + i - 3)
                        act.activation(ptb[:, i % 2, :], ps[:, i % 2, :], ACT.Copy).then_inc(sem("pt_ready"), 1)
                    if i - 3 in ENDS:
                        n, g = ENDS[i - 3]
                        act.wait_ge(sem("values_done"), g0 + i - 2)
                        act.activation(a_hi[:, 4 * g:4 * g + 4, n * P:(n + 1) * P], ps[:, 2 + g, :].rearrange("p (c q) -> p c q", q=P),
                                       ACT.Copy).then_inc(sem("att_hi"), 1)

            act.wait_ge(sem("par_ready"), 1)
            act.activation(csil[:, :], par[:, :, ROW[("c_2", 0)]], ACT.Silu).then_inc(sem("csil_ready"), 1)
            w.to(4)
            norm_squares("f0", h)
            turned_hi("f0")
            ffn_part(0)
            norm_squares("mix", h)
            turned_hi("mix")

            M = u_mix[0]
            for b in range(11):
                w.to(M + 4 * b + 6)
                if 1 <= b <= 4:
                    act.wait_ge(sem("conv_turned"), b)
                    j = b - 1
                    act.activation(uT[:, 2 * j:2 * j + 2, TAPS - 1:], ps[:, 4 + j % 2, :].rearrange("p (c n) -> p c n", c=2),
                                   ACT.Copy).then_inc(sem("uT_ready"), 1)
                w.to(M + 4 * b + 8)
                act.wait_ge(used, M + 4 * b + 4)
                for t in range(T):
                    if b < 4:
                        if b >= 2:
                            act.wait_ge(sem("cub_ready"), b - 1)
                        act.activation(csg[:, b % 2, t, :], acc(t, b % 2)[:, HALF:], ACT.Sigmoid).then_inc(sem("csg_ready"), 1)
                    elif b < 7:
                        c0 = 512 * (b - 4)
                        n = 512 if b < 6 else 256
                        act.activation(qkv[:, t, c0:c0 + n], acc(t, b % 2)[:, 0:n], ACT.Copy).then_inc(sem("mix_evac"), 1)
                    else:
                        c0 = 512 * (b - 7)
                        act.activation(gates[:, t, c0:c0 + 512], acc(t, b % 2), ACT.Sigmoid).then_inc(sem("mix_evac"), 1)
            for b in range(4):
                act.wait_ge(sem("q_turned"), b + 1)
                act.activation(qT[:, 2 * b:2 * b + 2, :].rearrange("p c n -> p (c n)"), ps[:, 4 + b, :], ACT.Copy).then_inc(sem("qT_ready"), 1)
            attention_part(0)
            w.to(u_cp + 4)
            act.wait_ge(sem("yc_ready"), 1)
            act.activation(ysq[:, :, :], y[:, :, :], ACT.Square).then_inc(sem("ysq_ready"), 1)
            act.wait_ge(sem("yn_ready"), 1)
            for c in range(KC):
                g, b = ROW[("conv_ln_g", 0)], ROW[("conv_ln_b", 0)]
                act.activation(cf[:, c, :], y[:, c, :], ACT.Silu, scale=par[:, c, g:g + 1], bias=par[:, c, b:b + 1]).then_inc(sem("cf_ready"), 1)
            w.to(u_wo + 4)
            turned_hi("merge")
            w.to(ffn[1][0] + 4)
            norm_squares("f1", h)
            turned_hi("f1")
            ffn_part(1)
            w.to(u_pp + 4)
            norm_squares("gate", h)
            act.wait_ge(sem("pin_turned"), 1)
            act.activation(b_hi[:, 0:2, :].rearrange("p c n -> p (c n)"), ps[:, 4, :], ACT.Copy).then_inc(sem("pin_hi"), 1)
            turned_hi("gate")
            w.to(u_pg + 4)
            act.wait_ge(used, u_pg)
            post_squares("emb", emb)
            w.to(u_pg + KC + 4)
            act.wait_ge(used, u_pg + KC)
            for t in range(T):
                act.activation(h[:, t, :], wide(t), ACT.Sigmoid).then_inc(sem("gate_ready"), 1)
            norm_squares("f2", h)
            turned_hi("f2")
            ffn_part(2)
            act.wait_ge(used, ffn[2][1] + FC)
            post_squares("f2", h)
            norm_squares("mix2", h)
            turned_hi("mix2")

            def between(b):
                if b == 1:
                    act.wait_ge(sem("alow_turned"), 1)
                    act.activation(alT[:, :], ps[0:16, 6, 0:S], ACT.Copy).then_inc(sem("alT_ready"), 1)
                    act.wait_ge(sem("nf_ready"), 1)
                    act.activation(lf[:, 1, :, :], lf[:, 1, :, :], ACT.Exp).then_inc(sem("act_step"), 1)
                    act.wait_ge(sem("act_step"), 1)
                    act.activation(lf[:, 1, :, :], lf[:, 1, :, :], ACT.Ln, bias=1.0).then_inc(sem("lnf_ready"), 1)
                if b in (2, 3):
                    act.wait_ge(sem("z_turned"), b - 1)
                    dst = (qa if b == 2 else ka)[:, :, :].rearrange("p h n -> p (h n)")
                    act.activation(dst, ps[:, 4:6, :].rearrange("p b n -> p (b n)"), ACT.Copy).then_inc(sem("qka_ready"), 1)
                if b == 3:
                    act.wait_ge(sem("na_ready"), 1)
                    act.activation(la[:, :, :], la[:, :, :], ACT.Exp).then_inc(sem("act_step"), 1)
                    act.wait_ge(sem("act_step"), 2)
                    act.activation(la[:, :, :], la[:, :, :], ACT.Ln, bias=1.0).then_inc(sem("lna_ready"), 1)
                if 8 <= b <= 11:
                    act.wait_ge(sem("z_turned"), b - 5)
                    dst = qb if b < 10 else kb
                    for i in range(2):
                        h0 = 8 * (b % 2) + 2 * i
                        act.activation(dst[:, h0:h0 + 2, :].rearrange("p h n -> p (h n)"), ps[0:AUG, 4 + i, :], ACT.Copy)\
                           .then_inc(sem("qkb_act"), 1)

            w.to(M2 + 4)
            for b in range(13):
                u1 = u_mix2[b + 1]
                w.to(u1 + 2)
                between(b)
                w.to(u1 + 4)
                act.wait_ge(used, u1)
                for t in range(T):
                    src = acc(t, b % 2)
                    if b == 0:
                        i = act.activation(sm[:, t, :], src[:, 0:32], ACT.Copy)
                    elif b in (1, 2):
                        if b == 2:
                            act.wait_ge(sem("z_turned"), 1)
                        i = act.activation(zt[:, t, :], src, ACT.Copy, scale=GDK ** -0.5 if b == 1 else 1.0)
                    elif b in (3, 4):
                        i = act.activation(va[:, t, 512 * (b - 3):512 * (b - 2)], src, ACT.Copy)
                    elif b in (5, 6):
                        i = act.activation(ra[:, t, 512 * (b - 5):512 * (b - 4)], src, ACT.Silu)
                    elif b in (7, 8, 9, 10):
                        act.wait_ge(sem("z_turned"), b - 5)
                        i = act.activation(aug[:, t, :, 0:HD], src.rearrange("p (h d) -> p h d", d=HD), ACT.Copy,
                                           scale=HD ** -0.5 if b < 9 else 1.0)
                    else:
                        i = act.activation(vb[:, t, 512 * (b - 11):512 * (b - 10)], src, ACT.Copy)
                    i.then_inc(sem("mix2_evac"), 1)

            for i in range(1, NSTEP):
                act.wait_ge(sem("diff_ready"), i)
                act.activation(dd[:, :, :], dd[:, :, :], ACT.Exp, scale=1.0 / 16.0).then_inc(sem("decay_ready"), 1)
            for t in range(T):
                act.wait_ge(sem("gla_out"), t + 1)
                for q in range(GH):
                    act.activation((qd, kd)[t][:, q * GDV:(q + 1) * GDV], acc(t, q // 2)[:, (q % 2) * GDV:(q % 2 + 1) * GDV], ACT.Square,
                                   accum_out=ga_ss[:, 0, t * GH + q:t * GH + q + 1]).then_inc(sem("gla_squares"), 1)
            G = u_mix2[13]
            w.to(G + 4)
            turned_hi("oa", b_hi)
            for b in range(4):
                w.to(G + 4 * b + 8)
                act.wait_ge(used, G + 4 * b + 4)
                for t in range(T):
                    act.activation(gates2[:, t, 512 * b:512 * b + 512], acc(t, b % 2), ACT.Sigmoid).then_inc(sem("gates2_ready"), 1)
            attention_part(1)
            w.to(u_wo2 + 4)
            turned_hi("merge2")
            w.to(u_wo2 + KC + 4)
            act.wait_ge(used, u_wo2 + KC)
            post_squares("mix2", h)
            norm_squares("f3", h)
            turned_hi("f3")
            ffn_part(3)
            act.wait_ge(used, ffn[3][1] + FC)
            post_squares("f3", h)

        @block.vector
        def _(dve):
            def lo_part(u):
                _, nk, n = units[u]
                dve.wait_ge(hi_ready, u + 1)
                dve.tensor_tensor(w_lo[:, u % SPLIT, 0:nk * n], raw[:, u % RAW, 0:nk * n],
                                  w_hi[:, u % SPLIT, 0:nk * n].bitcast(F32), ALU.subtract).then_inc(lo_ready, 1)

            w = Stream(lo_part)
            steps = [0]

            def then(ins):
                steps[0] += 1
                ins.then_inc(sem("dve_step"), 1)
                dve.wait_ge(sem("dve_step"), steps[0])

            def rsqrt(dst, src, scale, tmp):
                v, a = tmp[0], tmp[1]
                then(dve.tensor_scalar(v, src, scale, EPS, ALU.mult, ALU.add))
                then(dve.tensor_scalar(a.bitcast(I32), v.bitcast(I32), 1, None, ALU.logical_shift_right))
                then(dve.tensor_scalar(dst.bitcast(I32), a.bitcast(I32), -1.0, 1597463007.0, ALU.mult, ALU.add))
                for _ in range(3):
                    then(dve.tensor_tensor(a, dst, dst, ALU.mult))
                    then(dve.scalar_tensor_tensor(a, a, -0.5, v, ALU.mult, ALU.mult))
                    then(dve.scalar_tensor_tensor(dst, a, 1.5, dst, ALU.add, ALU.mult))

            def small(r, n=2):
                return [rt[:, 0, 0:n], rt[:, 1, 0:n]]

            def normalise(key):
                q = NORM[key]
                dve.wait_ge(sem("ss_ready"), 2 * q + 2)
                rsqrt(rstd[:, :], ss[:, :], 1.0 / D, small(rt))
                for t in range(T):
                    dve.tensor_scalar(h[:, t, :], x[:, t, :], rstd[:, t:t + 1], None, ALU.mult).then_inc(sem("h_ready"), 1)

            def turned_lo(key, hi=a_hi, lo=a_lo):
                k = TURN[key]
                for c in range(KC):
                    dve.wait_ge(sem("act_hi"), 8 * k + c // 2 * 2 + 2)
                    src = ps[:, 4 + c // 2, (c % 2) * S:(c % 2 + 1) * S]
                    hf = hi[:, c, :].bitcast(F32)
                    if key in SCALE_ROW:
                        r = ROW[SCALE_ROW[key]]
                        i = dve.scalar_tensor_tensor(lo[:, c, :], src, par[:, c, r:r + 1], hf, ALU.mult, ALU.subtract)
                    elif key in MODS:
                        g = MODS[key]
                        then(dve.tensor_scalar(shifted(c), src, modA[:, g, c:c + 1], modB[:, g, c:c + 1], ALU.mult, ALU.add))
                        i = dve.tensor_tensor(lo[:, c, :], shifted(c), hf, ALU.subtract)
                    else:
                        i = dve.tensor_tensor(lo[:, c, :], src, hf, ALU.subtract)
                    i.then_inc(sem("act_lo"), 1)

            def shifted(c):
                return b_lo_f[:, (c % 2) * S:(c % 2 + 1) * S]

            def ffn_part(f):
                up, dn = ffn[f]
                for j in range(UPB):
                    w.to(up + 4 * j + 6)
                    if j >= 1:
                        hidden_lo(f, j - 1)
                    take_mods(FFN[f], j)
                    w.to(up + 4 * j + 8)
                    for t in range(T):
                        dve.wait_ge(sem("silu_ready"), 2 * (f * UPB + j) + t + 1)
                        if j >= 2:
                            dve.wait_ge(sem("hid_turned"), f * UPB + j - 1)
                        i = dve.tensor_tensor(hid[:, j % 2, t, :], sg[:, j % 2, t, :], acc(t, j % 2)[:, HALF:], ALU.mult)
                    i.then_inc(sem("hid_ready"), 1)
                hidden_lo(f, UPB - 1)
                take_mods(FFN[f], UPB)
                w.to(dn + FC + 4)

            def hidden_lo(f, j):
                dve.wait_ge(sem("hid_hi_ready"), f * UPB + j + 1)
                dst, hf = (b[:, 2 * j:2 * j + 2, :].rearrange("p c n -> p (c n)") for b in (hid_lo, hid_hi))
                dve.tensor_tensor(dst, ps[:, 4 + j % 2, :], hf.bitcast(F32), ALU.subtract).then_inc(sem("hid_lo_ready"), 1)

            def take_mods(key, j):
                for m in MOD_AT.get((key, j), ()):
                    dve.wait_ge(sem("mod_summed"), m + 1)
                    g, kind = m // 3, m % 3
                    if kind == 0:
                        i = dve.tensor_copy(modB[:, g, :], ps[:, 6, 0:KC])
                    elif kind == 1:
                        r = ROW[("g_pre_2", g)]
                        i = dve.scalar_tensor_tensor(modA[:, g, :], ps[:, 6, 0:KC], 1.0, par[:, :, r], ALU.add, ALU.mult)
                    else:
                        dve.wait_ge(sem("gpost_landed"), 48)
                        i = dve.scalar_tensor_tensor(GT[:, g, :], ps[:, 6:8, :].rearrange("p b n -> p (b n)"),
                                                     1.0 if g == 1 else 0.5, GT[:, g, :], ALU.mult, ALU.mult)
                    i.then_inc(sem("mod_taken"), 1)

            def add_post(key):
                n = POST[key]
                dve.wait_ge(sem("pss_ready"), 2 * n + 2)
                rsqrt(prs[:, :], pss[:, :], 1.0 / D, small(rt))
                for t in range(T):
                    then(dve.scalar_tensor_tensor(h[:, t, :], wide(t), prs[:, t:t + 1], GT[:, MODS[key], :], ALU.mult, ALU.mult))
                    dve.tensor_tensor(x[:, t, :], x[:, t, :], h[:, t, :], ALU.add).then_inc(sem("x_ready"), 1)
                dve.wait_ge(sem("x_ready"), x_count[key])

            x_count = {"f2": 10, "mix2": 12, "f3": 14}

            def attention_part(m):
                prb = pr if m == 0 else pr2
                g0 = NG * m
                scale = HD ** -0.5
                for i in range(NG + 3):
                    if i < NG:
                        n, h0, nh, nk = GROUPS[i]
                        L = nk * P
                        s = st[:, i % 2, :, :]
                        dve.wait_ge(sem("scores_ready"), g0 + i + 1)
                        src = ps[:, 4 + i % 4, 0:nh * L].rearrange("p (h k) -> p h k", k=L)
                        then(dve.tensor_reduce(s[:, 0, 0:nh], src, AX, ALU.max))
                        if m == 0:
                            then(dve.scalar_tensor_tensor(s[:, 0, 0:nh], s[:, 0, 0:nh], scale, sinkb[:, h0:h0 + nh], ALU.mult, ALU.max))
                            then(dve.tensor_tensor(s[:, 4, 0:nh], sinkb[:, h0:h0 + nh], s[:, 0, 0:nh], ALU.subtract))
                        dve.tensor_scalar(s[:, 1, 0:nh], s[:, 0, 0:nh], -1.0, None, ALU.mult).then_inc(sem("bias_ready"), 1)
                    if m == 0:
                        conv(CONV_IN_MIX + 9 * i, CONV_IN_MIX + 9 * (i + 1))
                    if 1 <= i <= NG:
                        j = i - 1
                        n, h0, nh, nk = GROUPS[j]
                        L = nk * P
                        s = st[:, j % 2, :, :]
                        dve.wait_ge(sem("exp_done"), exps(m, j))
                        den = s[:, 2, 0:nh]
                        if m == 0:
                            then(dve.tensor_tensor(s[:, 2, 0:nh], s[:, 2, 0:nh], s[:, 3, 0:nh], ALU.add))
                        then(dve.reciprocal(s[:, 5, 0:nh], den))
                        v = prb[:, j % 2, 0:nh * L].rearrange("p (h k) -> p h k", k=L)
                        dve.tensor_tensor(v, v, s[:, 5, 0:nh].unsqueeze(2).to_broadcast([P, nh, L]), ALU.mult).then_inc(sem("probs_ready"), 1)
                    if i - 3 in ENDS:
                        n, g = ENDS[i - 3]
                        dve.wait_ge(sem("att_hi"), 4 * m + 2 * n + g + 1)
                        sl = (slice(None), slice(4 * g, 4 * g + 4), slice(n * P, (n + 1) * P))
                        dve.tensor_tensor(a_lo[sl], ps[:, 2 + g, :].rearrange("p (c q) -> p c q", q=P), a_hi[sl].bitcast(F32),
                                          ALU.subtract).then_inc(sem("att_lo"), 1)

            def conv(i0, i1):
                for i in range(i0, min(i1, TAPS * KC)):
                    k, c = i // KC, i % KC
                    src = uT[:, c, k:k + S]
                    if k == 0:
                        r = ROW[("dw_b", 0)]
                        ins = dve.tensor_scalar(y[:, c, :], src, par[:, c, 0:1], par[:, c, r:r + 1], ALU.mult, ALU.add)
                    else:
                        dve.wait_ge(sem("conv_step"), i - KC + 1)
                        ins = dve.scalar_tensor_tensor(y[:, c, :], src, par[:, c, k:k + 1], y[:, c, :], ALU.mult, ALU.add)
                    ins.then_inc(sem("conv_step"), 1)

            def gate_product(buf, part, done, t):
                dve.tensor_tensor(buf[:, t, part * D:(part + 1) * D], wide(t), buf[:, t, part * D:(part + 1) * D], ALU.mult)\
                   .then_inc(sem(done), 1)

            def merge(buf, done):
                for t in range(T):
                    gate_product(buf, 1, done, t)
                    dve.wait_ge(sem(done), t + 1)
                    dve.tensor_tensor(buf[:, t, 0:D], buf[:, t, 0:D], buf[:, t, D:], ALU.add).then_inc(sem("h_ready"), 1)

            dve.wait_ge(sem("par_turned"), 1)
            dve.tensor_copy(par[:, :, :].rearrange("p c r -> p (c r)"), ps[:, 7, 0:KC * NROW]).then_inc(sem("par_ready"), 1)
            dve.wait_ge(sem("const_landed"), 16)
            dve.tensor_copy(identb[:, :], ident).then_inc(sem("mask_ready"), 1)
            dve.tensor_copy(maskD[:, :], const[:, C_D:C_D + P]).then_inc(sem("mask_ready"), 1)
            dve.tensor_copy(maskWD[:, 0:P], const[:, C_W:C_W + P]).then_inc(sem("mask_ready"), 1)
            dve.tensor_copy(maskWD[:, P:], const[:, C_D:C_D + P]).then_inc(sem("mask_ready"), 1)
            w.to(4)
            normalise("f0")
            turned_lo("f0")
            ffn_part(0)
            dve.wait_ge(used, ffn[0][1] + FC)
            for t in range(T):
                dve.scalar_tensor_tensor(x[:, t, :], wide(t), 0.5, x[:, t, :], ALU.mult, ALU.add).then_inc(sem("x_ready"), 1)
            dve.wait_ge(sem("x_ready"), 2)
            normalise("mix")
            turned_lo("mix")

            M = u_mix[0]
            then(dve.memset(uT[:, :, 0:TAPS - 1], 0.0))
            for b in range(11):
                slot = [M + 4 * b + 5 + i for i in range(4)]
                w.to(slot[1])
                if b >= 5:
                    conv(24 * (b - 5), 24 * (b - 5) + 12)
                take_mods("mix", b)
                w.to(slot[3])
                if b < 4:
                    for t in range(T):
                        dve.wait_ge(sem("csg_ready"), 2 * b + t + 1)
                        if b >= 2:
                            dve.wait_ge(sem("conv_turned"), b - 1)
                        i = dve.tensor_tensor(cub[:, b % 2, t, :], acc(t, b % 2)[:, 0:HALF], csg[:, b % 2, t, :], ALU.mult)
                    i.then_inc(sem("cub_ready"), 1)
                if b == 4:
                    dve.wait_ge(sem("uT_ready"), 4)
                if b >= 5:
                    conv(24 * (b - 5) + 12, 24 * (b - 5) + 24)
                if b in (7, 8):
                    t = b - 7
                    dve.wait_ge(sem("mix_evac"), 6)
                    if t == 0:
                        dve.wait_ge(sem("small_landed"), 96)
                    z = qkv[:, t, 0:18 * HD].rearrange("p (h d) -> p h d", d=HD)
                    sq = qsq[:, :].rearrange("p (h d) -> p h d", d=HD)
                    then(dve.tensor_tensor(sq, z, z, ALU.mult))
                    then(dve.tensor_reduce(rt[:, 2, 0:18], sq, AX, ALU.add))
                    rsqrt(rs18[:, :], rt[:, 2, 0:18], 1.0 / HD, small(rt, 18))
                    then(dve.tensor_tensor(z, z, rs18[:, :].unsqueeze(2).to_broadcast([P, 18, HD]), ALU.mult))
                    then(dve.tensor_tensor(z[:, 0:NH, :], z[:, 0:NH, :], gq[:, :].unsqueeze(1).to_broadcast([P, NH, HD]), ALU.mult))
                    then(dve.tensor_tensor(z[:, NH:, :], z[:, NH:, :], gk[:, :].unsqueeze(1).to_broadcast([P, 2, HD]), ALU.mult))
                    cos = const[:, C_COS + 8 * t:C_COS + 8 * t + 8].unsqueeze(1).to_broadcast([P, 18, 8])
                    sin = const[:, C_SIN + 8 * t:C_SIN + 8 * t + 8].unsqueeze(1).to_broadcast([P, 18, 8])
                    for n, (part, table) in enumerate([(0, cos), (1, sin), (1, cos), (0, sin)]):
                        then(dve.tensor_tensor(rope[:, n, :, :], z[:, :, 8 * part:8 * part + 8], table, ALU.mult))
                    then(dve.tensor_tensor(z[:, :, 0:8], rope[:, 0, :, :], rope[:, 1, :, :], ALU.subtract))
                    then(dve.tensor_tensor(z[:, :, 8:16], rope[:, 2, :, :], rope[:, 3, :, :], ALU.add))
                    for g in range(2):
                        dve.tensor_copy(kdup[:, t, g, :, :], z[:, NH + g, :].unsqueeze(1).to_broadcast([P, 2, HD])).then_inc(sem("qk_ready"), 1)
            then(dve.memset(kTz[:, :, :, :], 0.0))
            dve.wait_ge(sem("k_turned"), 1)
            for g in range(2):
                for half in range(2):
                    r = slice(half * HD, (half + 1) * HD)
                    dve.tensor_copy(kTz[r, g, half, :], ps[r, 0, g * S:(g + 1) * S]).then_inc(sem("kT_ready"), 1)
            attention_part(0)
            conv(CONV_IN_MIX + 9 * (NG + 3), TAPS * KC)
            w.to(u_cp + 4)
            dve.wait_ge(used, u_cp)
            for t in range(T):
                gate_product(gates, 0, "gated_a", t)
            dve.wait_ge(sem("conv_step"), TAPS * KC)
            dve.wait_ge(sem("y_summed"), 1)
            then(dve.tensor_scalar(lnb[:, 0, :], ps[:, 4, 0:S], 1.0 / D, None, ALU.mult))
            dve.tensor_tensor(y[:, :, :], y[:, :, :], lnb[:, 0, :].unsqueeze(1).to_broadcast([P, KC, S]), ALU.subtract)\
               .then_inc(sem("yc_ready"), 1)
            dve.wait_ge(sem("y_summed"), 2)
            rsqrt(lnb[:, 1, :], ps[:, 5, 0:S], 1.0 / D, [lnt[:, 0, :], lnt[:, 1, :]])
            dve.tensor_tensor(y[:, :, :], y[:, :, :], lnb[:, 1, :].unsqueeze(1).to_broadcast([P, KC, S]), ALU.mult)\
               .then_inc(sem("yn_ready"), 1)
            for c in range(KC):
                dve.wait_ge(sem("cf_ready"), c + 1)
                then(dve.tensor_copy(b_hi[:, c, :], cf[:, c, :]))
                dve.tensor_tensor(b_lo[:, c, :], cf[:, c, :], b_hi[:, c, :].bitcast(F32), ALU.subtract).then_inc(sem("b_ready"), 1)
            w.to(u_wo + 4)
            dve.wait_ge(used, u_wo)
            merge(gates, "gated_b")
            turned_lo("merge")
            w.to(ffn[1][0] + 4)
            dve.wait_ge(used, ffn[1][0])
            for t in range(T):
                dve.tensor_tensor(x[:, t, :], wide(t), x[:, t, :], ALU.add).then_inc(sem("x_ready"), 1)
            dve.wait_ge(sem("x_ready"), 4)
            normalise("f1")
            turned_lo("f1")
            ffn_part(1)
            dve.wait_ge(used, ffn[1][1] + FC)
            for t in range(T):
                dve.scalar_tensor_tensor(x[:, t, :], wide(t), 0.5, x[:, t, :], ALU.mult, ALU.add).then_inc(sem("x_ready"), 1)
            dve.wait_ge(sem("x_ready"), 6)
            normalise("gate")
            dve.wait_ge(sem("pin_hi"), 1)
            dve.tensor_tensor(b_lo[:, 0:2, :].rearrange("p c n -> p (c n)"), ps[:, 4, :],
                              b_hi[:, 0:2, :].rearrange("p c n -> p (c n)").bitcast(F32), ALU.subtract).then_inc(sem("pin_lo"), 1)
            turned_lo("gate")
            w.to(u_pg + 4)
            dve.wait_ge(sem("pss_ready"), 2)
            dve.wait_ge(sem("grow_landed"), 16)
            rsqrt(prs[:, :], pss[:, :], 1.0 / D, small(rt))
            for t in range(T):
                dve.scalar_tensor_tensor(emb[:, t, :], wide(t), prs[:, t:t + 1], grow[:, :], ALU.mult, ALU.mult).then_inc(sem("emb_ready"), 1)
            w.to(u_pg + KC + 4)
            for t in range(T):
                dve.wait_ge(sem("gate_ready"), t + 1)
                then(dve.tensor_tensor(h[:, t, :], h[:, t, :], emb[:, t, :], ALU.mult))
                dve.tensor_tensor(x[:, t, :], x[:, t, :], h[:, t, :], ALU.add).then_inc(sem("x_ready"), 1)
            dve.wait_ge(sem("x_ready"), 8)
            normalise("f2")
            turned_lo("f2")
            ffn_part(2)
            add_post("f2")
            normalise("mix2")
            turned_lo("mix2")

            w.to(M2 + 4)
            for b in range(13):
                u1 = u_mix2[b + 1]
                w.to(u1 + 2)
                if b == 1:
                    dve.wait_ge(sem("mix2_evac"), 2)
                    then(dve.tensor_tensor(lf[:, 0, :, :], sm[:, :, 16:32], bfb[:, :].unsqueeze(1).to_broadcast([P, T, NH]), ALU.add))
                    dve.scalar_tensor_tensor(lf[:, 1, :, :], lf[:, 0, :, :], -1.0, lf[:, 0, :, :], ALU.mult, ALU.min).then_inc(sem("nf_ready"), 1)
                if b == 2:
                    dve.wait_ge(sem("lnf_ready"), 1)
                    dve.scalar_tensor_tensor(lf[:, 2, :, :], lf[:, 0, :, :], 0.0, lf[:, 1, :, :], ALU.min, ALU.subtract).then_inc(sem("lf_ready"), 1)
                    dve.wait_ge(sem("decay_product"), 1)
                    for q in range(GH):
                        i = dve.tensor_scalar(ya[:, q, :], ps[:, 6 + q // 2, (q % 2) * S:(q % 2 + 1) * S], baT[:, q:q + 1], None, ALU.add)
                    then(i)
                    dve.scalar_tensor_tensor(la[:, :, :], ya[:, :, :], -1.0, ya[:, :, :], ALU.mult, ALU.min).then_inc(sem("na_ready"), 1)
                if b == 3:
                    dve.wait_ge(sem("F_summed"), 1)
                    dve.tensor_copy(Fc[:, :, :].rearrange("p t h -> p (t h)"), ps[:, 6, 0:T * NH]).then_inc(sem("F_ready"), 1)
                if b == 4:
                    dve.wait_ge(sem("lna_ready"), 1)
                    then(dve.scalar_tensor_tensor(la[:, :, :], ya[:, :, :], 0.0, la[:, :, :], ALU.min, ALU.subtract))
                    for q in range(GH):
                        dve.tensor_tensor_scan(bc[:, q, :], ones[:, 0:1].to_broadcast([P, S]), la[:, q, :], 0.0, ALU.mult, ALU.add)\
                           .then_inc(sem("bc_ready"), 1)
                if 8 <= b <= 11:
                    dve.wait_ge(sem("z_turned"), b - 5)
                    dst = qb if b < 10 else kb
                    for i in range(2, 4):
                        h0 = 8 * (b % 2) + 2 * i
                        dve.tensor_copy(dst[:, h0:h0 + 2, :].rearrange("p h n -> p (h n)"), ps[0:AUG, 4 + i, :]).then_inc(sem("qkb_dve"), 1)
                w.to(u1 + 4)
                if 7 <= b <= 10:
                    dve.wait_ge(sem("z_turned"), b - 5)
                    if b == 7:
                        dve.wait_ge(sem("F_ready"), 1)
                    f = Fc[:, :, 8 * ((b - 7) % 2):8 * ((b - 7) % 2) + 8]
                    one, col, sign = (HD, HD + 1, 1.0) if b < 9 else (HD + 1, HD, -1.0)
                    dve.memset(aug[:, :, :, one], 1.0).then_inc(sem("aug_ready"), 1)
                    dve.tensor_scalar(aug[:, :, :, col], f, sign, None, ALU.mult).then_inc(sem("aug_ready"), 1)

            dve.wait_ge(sem("z_turned"), 6)
            dve.wait_ge(sem("qka_ready"), 2)
            dve.wait_ge(sem("glam_landed"), 32)
            dve.wait_ge(sem("bc_ready"), GH)
            then(dve.memset(qd[:, :], 0.0))
            then(dve.memset(kd[:, :], 0.0))
            qf, kf, bf = (b_[:, :, :].rearrange("p h n -> p (h n)") for b_ in (qa, ka, bc))

            def masked(i):
                dve.wait_ge(sem("gla_scores"), i + 1)
                if i == NSTEP - 1:
                    dve.tensor_copy(AT[:, 2, :, :].rearrange("p h n -> p (h n)"), ps[:, 4, :]).then_inc(sem("gla_masked"), 1)
                    return
                m = glam[:, i, :].unsqueeze(1).to_broadcast([P, GH, P])
                for tile in range(T):
                    src = ps[:, 4 + 2 * (i % 2) + tile, :].rearrange("p (h n) -> p h n", n=P)
                    if i == 0:
                        ins = dve.tensor_tensor(AT[:, tile, :, :], src, m, ALU.mult)
                    else:
                        tmp = gtmp[:, :].rearrange("p (h n) -> p h n", n=P)
                        then(dve.tensor_tensor(tmp, src, m, ALU.mult))
                        ins = dve.tensor_tensor(AT[:, tile, :, :], AT[:, tile, :, :], tmp, ALU.add)
                    if tile == T - 1:
                        ins.then_inc(sem("gla_masked"), 1)
                    else:
                        then(ins)
                dve.wait_ge(sem("gla_masked"), i + 1)

            for i in range(1, NSTEP):
                L = (LEVELS + [P])[i - 1]

                def blocks(a, side):
                    return a.rearrange("p (b s l) -> p b s l", s=2, l=L)[:, :, side, :]

                n = GH * S // (2 * L)
                last = bf.rearrange("p (b s l) -> p b s l", s=2, l=L)[:, :, 0, L - 1:L].to_broadcast([P, n, L])
                d = [dd[:, s, :].rearrange("p (b l) -> p b l", l=L) for s in range(2)]
                then(dve.tensor_tensor(d[0], blocks(bf, 1), last, ALU.subtract))
                dve.tensor_tensor(d[1], last, blocks(bf, 0), ALU.subtract).then_inc(sem("diff_ready"), 1)
                masked(i - 1)
                dve.wait_ge(sem("decay_ready"), i)
                then(dve.tensor_tensor(blocks(qd[:, :], 1), blocks(qf, 1), d[0], ALU.mult))
                dve.tensor_tensor(blocks(kd[:, :], 0), blocks(kf, 0), d[1], ALU.mult).then_inc(sem("decayed"), 1)
            masked(NSTEP - 1)
            dve.wait_ge(sem("gla_squares"), T * GH)
            rsqrt(ga_ss[:, 1, :], ga_ss[:, 0, :], 1.0 / GDV, [ga_ss[:, 2, :], ga_ss[:, 3, :]])
            for t in range(T):
                for q in range(GH):
                    c = slice(q * GDV, (q + 1) * GDV)
                    i = dve.scalar_tensor_tensor(va[:, t, c], acc(t, q // 2)[:, (q % 2) * GDV:(q % 2 + 1) * GDV],
                                                 ga_ss[:, 1, t * GH + q:t * GH + q + 1], ggla[:, c], ALU.mult, ALU.mult)
                    if q == GH - 1:
                        then(i)
                dve.tensor_tensor(va[:, t, :], va[:, t, :], ra[:, t, :], ALU.mult).then_inc(sem("h_ready"), 1)
            G = u_mix2[13]
            w.to(G + 4)
            turned_lo("oa", b_hi, b_lo)
            for b in range(4):
                w.to(G + 4 * b + 8)
            attention_part(1)
            w.to(u_pb + 4)
            dve.wait_ge(used, u_pb)
            for t in range(T):
                gate_product(gates2, 0, "gated2_a", t)
            w.to(u_wo2 + 4)
            dve.wait_ge(used, u_wo2)
            merge(gates2, "gated2_b")
            turned_lo("merge2")
            w.to(u_wo2 + KC + 4)
            add_post("mix2")
            normalise("f3")
            turned_lo("f3")
            ffn_part(3)
            add_post("f3")

        @block.tensor
        def _(pe):
            def slot(u, buf, kk, n, c0=0, c1=None):
                a = buf[:, u % SPLIT, kk * n:(kk + 1) * n]
                return a[:, c0:c1 if c1 is not None else n]

            def col_unit(u, k0, dst, hi=a_hi, lo=a_lo):
                _, nk, n = units[u]
                pe.wait_ge(lo_ready, u + 1)
                for kk in range(nk):
                    kc = k0 + kk
                    for t in range(T):
                        a = [v[:, kc, t * P:(t + 1) * P] for v in (hi, lo)]
                        pe.matmul(dst(t)[:, 0:n], a[0], slot(u, w_hi, kk, n), start=kc == 0, stop=False)
                        pe.matmul(dst(t)[:, 0:n], a[0], slot(u, w_lo, kk, n), start=False, stop=False)
                        i = pe.matmul(dst(t)[:, 0:n], a[1], slot(u, w_hi, kk, n), start=False, stop=kc == KC - 1)
                i.then_inc(used, 1)

            def row_unit(u, kc, last, hi, lo):
                pe.wait_ge(lo_ready, u + 1)
                for t in range(T):
                    a = [v[:, kc, t * P:(t + 1) * P] for v in (hi, lo)]
                    for x_, w_ in ((0, w_hi), (0, w_lo), (1, w_hi)):
                        for n in range(2):
                            i = pe.matmul(acc(t, n), a[x_], slot(u, w_, 0, D, 512 * n, 512 * (n + 1)),
                                          start=kc == 0 and x_ == 0 and w_ is w_hi, stop=kc == last and x_ == 1)
                i.then_inc(used, 1)

            def turn(key, src):
                k = TURN[key]
                pe.wait_ge(sem("h_ready"), 2 * k + 2)
                for b in range(4):
                    for c in range(2 * b, 2 * b + 2):
                        for t in range(T):
                            i = pe.transpose(ps[:, 4 + b, (c % 2) * S + t * P:(c % 2) * S + (t + 1) * P], src[:, t, c * P:(c + 1) * P], ident)
                    i.then_inc(sem("turned"), 1)

            def act_ready(key, kc):
                pe.wait_ge(sem("act_lo"), 8 * TURN[key] + kc + 1)

            def ffn_part(f):
                up, dn = ffn[f]
                for j in range(UPB):
                    if j >= 2:
                        pe.wait_ge(sem("hid_ready"), f * UPB + j - 1)
                    for i in range(4):
                        if j == 0:
                            act_ready(FFN[f], 2 * i + 1)
                        col_unit(up + 4 * j + i, 2 * i, lambda t: acc(t, j % 2))
                        if i == 1:
                            if j >= 1:
                                turn_hidden(f, j - 1)
                            sum_mods(FFN[f], j)
                turn_hidden(f, UPB - 1)
                sum_mods(FFN[f], UPB)
                for k in range(FC):
                    pe.wait_ge(sem("hid_lo_ready"), f * UPB + k // 2 + 1)
                    row_unit(dn + k, k, FC - 1, hid_hi, hid_lo)

            def turn_hidden(f, j):
                pe.wait_ge(sem("hid_ready"), f * UPB + j + 1)
                if j >= 2:
                    pe.wait_ge(sem("hid_lo_ready"), f * UPB + j - 1)
                for c in range(2):
                    for t in range(T):
                        i = pe.transpose(ps[:, 4 + j % 2, c * S + t * P:c * S + (t + 1) * P], hid[:, j % 2, t, c * P:(c + 1) * P], ident)
                i.then_inc(sem("hid_turned"), 1)

            def sum_mods(key, j):
                for m in MOD_AT.get((key, j), ()):
                    pe.wait_ge(sem("mod_ready"), m + 1)
                    if m >= 1:
                        pe.wait_ge(sem("mod_taken"), m)
                    if m % 3 == 2:
                        for n in range(2):
                            i = pe.matmul(ps[:, 6 + n, :], ones, acc_m[:, m % 2, 512 * n:512 * (n + 1)], start=True, stop=True)
                    else:
                        for c in range(KC):
                            i = pe.matmul(ps[:, 6, c:c + 1], acc_m[:, m % 2, c * P:(c + 1) * P], ones[:, 0:1], start=True, stop=True)
                    i.then_inc(sem("mod_summed"), 1)

            def attention_part(m):
                prb, ptb = (pr, pt) if m == 0 else (pr2, pt2)
                g0 = NG * m

                def scores(i):
                    n, h0, nh, nk = GROUPS[i]
                    L = nk * P
                    bank = ps[:, 4 + i % 4, :]
                    if i >= 4:
                        pe.wait_ge(sem("exp_done"), exps(m, i - 4))
                    if m == 0:
                        mask = maskD[:, :] if n == 0 else maskWD[:, :]
                        pe.matmul(bank.rearrange("p (h k) -> p h k", k=L), identb[:, :], mask.unsqueeze(1).to_broadcast([P, nh, L]),
                                  start=True, stop=True)
                    else:
                        v = bank.rearrange("p (h k) -> p h k", k=L)[:, :, (nk - 1) * P:]
                        pe.matmul(v, identb[:, :], maskD[:, :].unsqueeze(1).to_broadcast([P, nh, P]), start=True, stop=True,
                                  skip_group_check=True)
                    for q in range(nh):
                        hh = h0 + q
                        if m == 0:
                            lhs, rhs = qT[:, hh // 2, n * P:(n + 1) * P], kTz[:, hh // 8, hh % 2, 0:L]
                        else:
                            lhs, rhs = qb[:, hh, n * P:(n + 1) * P], kb[:, hh, 0:L]
                        i_ = pe.matmul(bank[:, q * L:(q + 1) * L], lhs, rhs, start=False, stop=True, skip_group_check=True)
                    i_.then_inc(sem("scores_ready"), 1)

                def turn_probs(i):
                    pe.wait_ge(sem("probs_ready"), g0 + i + 1)
                    if i >= 2:
                        pe.wait_ge(sem("pt_ready"), g0 + i - 1)
                    for q in range(4):
                        i_ = pe.transpose(ps[:, i % 2, q * P:(q + 1) * P], prb[:, i % 2, q * P:(q + 1) * P], ident)
                    i_.then_inc(sem("probs_turned"), 1)

                def values(i):
                    n, h0, nh, nk = GROUPS[i]
                    pe.wait_ge(sem("pt_ready"), g0 + i + 1)
                    if n == 1 and h0 in (0, 8):
                        pe.wait_ge(sem("att_lo"), 4 * m + h0 // 8 + 1)
                    for q in range(nh):
                        hh = h0 + q
                        r = (hh % 2) * HD
                        dst = ps[r:r + HD, 2 + hh // 8, (hh % 8 // 2) * P:(hh % 8 // 2 + 1) * P]
                        for k in range(nk):
                            if m == 0:
                                v = qkv[:, k, 18 * HD + (hh // 8) * HD:18 * HD + (hh // 8 + 1) * HD]
                            else:
                                v = vb[:, k, hh * HD:(hh + 1) * HD]
                            c = (q * nk + k) * P
                            i_ = pe.matmul(dst, v, ptb[:, i % 2, c:c + P], start=k == 0, stop=k == nk - 1)
                    i_.then_inc(sem("values_done"), 1)

                for i in range(NG + 3):
                    if i < NG:
                        scores(i)
                    if 2 <= i < NG + 2:
                        turn_probs(i - 2)
                    if i >= 3:
                        values(i - 3)

            pe.wait_ge(sem("const_landed"), 16)
            pe.wait_ge(sem("prow_landed"), 16 * (NROW - TAPS + 1))
            for c in range(KC):
                i = pe.transpose(ps[:, 7, c * NROW:(c + 1) * NROW], prow[:, c * P:(c + 1) * P], ident[0:NROW, 0:NROW])
            i.then_inc(sem("par_turned"), 1)
            pe.wait_ge(sem("par_ready"), 1)
            turn("f0", h)
            ffn_part(0)
            turn("mix", h)

            M = u_mix[0]
            for b in range(11):
                if 2 <= b < 6:
                    pe.wait_ge(sem("cub_ready"), b - 1)
                elif b >= 6:
                    pe.wait_ge(sem("mix_evac"), 2 * (b - 5))
                for i in range(4):
                    if b == 0:
                        act_ready("mix", 2 * i + 1)
                    col_unit(M + 4 * b + i, 2 * i, lambda t: acc(t, b % 2))
                    if i == 1:
                        if 1 <= b <= 4:
                            j = b - 1
                            pe.wait_ge(sem("cub_ready"), j + 1)
                            if j >= 2:
                                pe.wait_ge(sem("uT_ready"), j - 1)
                            for c in range(2):
                                for t in range(T):
                                    ins = pe.transpose(ps[:, 4 + j % 2, c * S + t * P:c * S + (t + 1) * P],
                                                       cub[:, j % 2, t, c * P:(c + 1) * P], ident)
                            ins.then_inc(sem("conv_turned"), 1)
                        sum_mods("mix", b)
            pe.wait_ge(sem("mod_taken"), 4)
            pe.wait_ge(sem("qk_ready"), 4)
            for b in range(4):
                for c in range(2 * b, 2 * b + 2):
                    for t in range(T):
                        i = pe.transpose(ps[:, 4 + b, (c % 2) * S + t * P:(c % 2) * S + (t + 1) * P], qkv[:, t, c * P:(c + 1) * P], ident)
                i.then_inc(sem("q_turned"), 1)
            pe.wait_ge(sem("mix_evac"), 14)
            for g in range(2):
                for t in range(T):
                    i = pe.transpose(ps[:, 0, g * S + t * P:g * S + (t + 1) * P], kdup[:, t, g, :, :].rearrange("p a d -> p (a d)"), ident)
            i.then_inc(sem("k_turned"), 1)
            pe.wait_ge(sem("kT_ready"), 4)
            pe.wait_ge(sem("qT_ready"), 4)
            pe.wait_ge(sem("mask_ready"), 4)
            attention_part(0)
            pe.wait_ge(sem("att_lo"), 4)
            for k in range(KC):
                row_unit(u_ap + k, k, KC - 1, a_hi, a_lo)
            pe.wait_ge(sem("conv_step"), TAPS * KC)
            for c in range(KC):
                i = pe.matmul(ps[:, 4, 0:S], ones, y[:, c, :], start=c == 0, stop=c == KC - 1)
            i.then_inc(sem("y_summed"), 1)
            pe.wait_ge(sem("ysq_ready"), 1)
            for c in range(KC):
                i = pe.matmul(ps[:, 5, 0:S], ones, ysq[:, c, :], start=c == 0, stop=c == KC - 1)
            i.then_inc(sem("y_summed"), 1)
            pe.wait_ge(sem("gated_a"), 2)
            for k in range(KC):
                pe.wait_ge(sem("b_ready"), k + 1)
                row_unit(u_cp + k, k, KC - 1, b_hi, b_lo)
            turn("merge", gates)
            for k in range(KC):
                act_ready("merge", k)
                row_unit(u_wo + k, k, KC - 1, a_hi, a_lo)
            turn("f1", h)
            ffn_part(1)
            pe.wait_ge(sem("pin_landed"), 16)
            for c in range(2):
                for t in range(T):
                    i = pe.transpose(ps[:, 4, c * S + t * P:c * S + (t + 1) * P], pin[:, t, c * P:(c + 1) * P], ident)
            i.then_inc(sem("pin_turned"), 1)
            pe.wait_ge(sem("pin_lo"), 1)
            pe.wait_ge(sem("x_ready"), 6)
            for k in range(2):
                row_unit(u_pp + k, k, 1, b_hi, b_lo)
            turn("gate", h)
            pe.wait_ge(sem("emb_ready"), 2)
            for k in range(KC):
                act_ready("gate", k)
                row_unit(u_pg + k, k, KC - 1, a_hi, a_lo)
            turn("f2", h)
            ffn_part(2)
            turn("mix2", h)

            for b in range(13):
                u0 = u_mix2[b]
                if b >= 2:
                    pe.wait_ge(sem("mix2_evac"), 2 * (b - 1))
                if b == 0:
                    act_ready("mix2", KC - 1)
                    col_unit(u0, 0, lambda t: acc(t, 0))
                    continue
                for i in range(4):
                    col_unit(u0 + i, 2 * i, lambda t: acc(t, b % 2))
                    if i != 1:
                        continue
                    if b == 1:
                        pe.wait_ge(sem("mix2_evac"), 2)
                        for t in range(T):
                            ins = pe.transpose(ps[0:16, 6, t * P:(t + 1) * P], sm[:, t, 0:16], ident)
                        ins.then_inc(sem("alow_turned"), 1)
                    if b in (2, 3):
                        pe.wait_ge(sem("mix2_evac"), 2 * b)
                        if b == 3:
                            pe.wait_ge(sem("qka_ready"), 1)
                        for q in range(GH):
                            for t in range(T):
                                ins = pe.transpose(ps[:, 4 + q // 2, (q % 2) * S + t * P:(q % 2) * S + (t + 1) * P],
                                                   zt[:, t, q * P:(q + 1) * P], ident)
                        ins.then_inc(sem("z_turned"), 1)
                    if b == 2:
                        pe.wait_ge(sem("alT_ready"), 1)
                        for q in range(GH):
                            ins = pe.matmul(ps[:, 6 + q // 2, (q % 2) * S:(q % 2 + 1) * S], wa2[:, q * P:(q + 1) * P], alT[:, :],
                                            start=True, stop=True)
                        ins.then_inc(sem("decay_product"), 1)
                    if b == 3:
                        pe.wait_ge(sem("lf_ready"), 1)
                        pe.wait_ge(sem("na_ready"), 1)
                        tri = const[:, C_TRI:C_TRI + P]
                        pe.matmul(ps[:, 6, 0:NH], tri, lf[:, 2, 0, :], start=True, stop=True)
                        pe.matmul(ps[:, 6, NH:2 * NH], ones, lf[:, 2, 0, :], start=True, stop=False)
                        pe.matmul(ps[:, 6, NH:2 * NH], tri, lf[:, 2, 1, :], start=False, stop=True).then_inc(sem("F_summed"), 1)
                    if 8 <= b <= 11:
                        pe.wait_ge(sem("mix2_evac"), 2 * b)
                        pe.wait_ge(sem("aug_ready"), 2 * (b - 7))
                        if b == 8:
                            pe.wait_ge(sem("qka_ready"), 2)
                            pe.wait_ge(sem("F_ready"), 1)
                        else:
                            pe.wait_ge(sem("qkb_act"), 2 * (b - 8))
                            pe.wait_ge(sem("qkb_dve"), 2 * (b - 8))
                        for q in range(8):
                            for t in range(T):
                                ins = pe.transpose(ps[0:AUG, 4 + q // 2, (q % 2) * S + t * P:(q % 2) * S + (t + 1) * P],
                                                   aug[:, t, q, :], ident)
                        ins.then_inc(sem("z_turned"), 1)

            pe.wait_ge(sem("qkb_act"), 8)
            pe.wait_ge(sem("qkb_dve"), 8)
            for i in range(NSTEP):
                if i >= 1:
                    pe.wait_ge(sem("decayed"), i)
                if i >= 2:
                    pe.wait_ge(sem("gla_masked"), i - 1)
                if i == NSTEP - 1:
                    for q in range(GH):
                        ins = pe.matmul(ps[:, 4, q * P:(q + 1) * P], kd[:, q * S:q * S + P], qd[:, q * S + P:(q + 1) * S], start=True, stop=True)
                else:
                    for tile in range(T):
                        for q in range(GH):
                            c = slice(q * S + tile * P, q * S + (tile + 1) * P)
                            k_, q_ = ((ka, qa) if i == 0 else (kd, qd))
                            if i == 0:
                                k_, q_ = (v[:, q, tile * P:(tile + 1) * P] for v in (ka, qa))
                            else:
                                k_, q_ = kd[:, c], qd[:, c]
                            ins = pe.matmul(ps[:, 4 + 2 * (i % 2) + tile, q * P:(q + 1) * P], k_, q_, start=True, stop=True)
                ins.then_inc(sem("gla_scores"), 1)
            pe.wait_ge(sem("gla_masked"), NSTEP)
            pe.wait_ge(sem("mix2_evac"), 26)
            for t in range(T):
                for q in range(GH):
                    dst = acc(t, q // 2)[:, (q % 2) * GDV:(q % 2 + 1) * GDV]
                    v = [va[:, s, q * GDV:(q + 1) * GDV] for s in range(T)]
                    if t == 0:
                        ins = pe.matmul(dst, AT[:, 0, q, :], v[0], start=True, stop=True)
                    else:
                        pe.matmul(dst, AT[:, 2, q, :], v[0], start=True, stop=False)
                        ins = pe.matmul(dst, AT[:, 1, q, :], v[1], start=False, stop=True)
                ins.then_inc(sem("gla_out"), 1)
            turn("oa", va)
            G = u_mix2[13]
            for b in range(4):
                if b >= 2:
                    pe.wait_ge(sem("gates2_ready"), 2 * (b - 1))
                for i in range(4):
                    col_unit(G + 4 * b + i, 2 * i, lambda t: acc(t, b % 2))
            pe.wait_ge(sem("gates2_ready"), 8)
            pe.wait_ge(sem("act_lo"), 8 * TURN["oa"] + 8)
            attention_part(1)
            pe.wait_ge(sem("att_lo"), 8)
            for k in range(KC):
                row_unit(u_pa + k, k, KC - 1, b_hi, b_lo)
            pe.wait_ge(sem("gated2_a"), 2)
            for k in range(KC):
                row_unit(u_pb + k, k, KC - 1, a_hi, a_lo)
            turn("merge2", gates2)
            for k in range(KC):
                act_ready("merge2", k)
                row_unit(u_wo2 + k, k, KC - 1, a_hi, a_lo)
            turn("f3", h)
            ffn_part(3)


_INS = ["x", "p", "ffn1_norm", "ffn1_wgu", "ffn1_wdown", "mix_norm", "w_in", "q_norm", "k_norm", "sinks", "attn_proj",
        "dw_w", "dw_b", "conv_ln_g", "conv_ln_b", "conv_proj", "w_out", "ffn2_norm", "ffn2_wgu", "ffn2_wdown",
        "ple_proj", "ple_norm", "ple_gate_norm", "ple_gate_w", "c_2", "w_ada_2", "b_ada_2", "g_pre_2", "g_post_2",
        "w_gu1_2", "w_dn1_2", "w_gu2_2", "w_dn2_2", "w_in_2", "w_a2_2", "b_a_2", "b_f_2", "g_gla_2", "w_pa_2", "w_pb_2",
        "w_out_2"]


def kernel(**inputs):
    import numpy as _np
    import concourse.bacc as _bacc
    from concourse import mybir as _mybir
    from concourse.bass_utils import run_bass_kernel_spmd as _run

    nc = _bacc.Bacc("TRN2", target_bir_lowering=False, num_devices=1)
    arrays, args = {}, {}
    for name in _INS:
        a = _np.ascontiguousarray(inputs[name])
        arrays[f"in_{name}_dram"] = a
        args[name] = nc.dram_tensor(f"in_{name}_dram", a.shape, _mybir.dt.from_np(a.dtype), kind="ExternalInput").ap()
    table = shape_constants()
    arrays["shape_constants_dram"] = table
    consts = nc.dram_tensor("shape_constants_dram", table.shape, _mybir.dt.float32, kind="ExternalInput").ap()
    out = nc.dram_tensor("out_0_dram", (1, S, D), _mybir.dt.float32, kind="ExternalOutput").ap()
    two_blocks(nc, args, consts, out)
    r = _run(nc, [arrays], core_ids=[0])
    return r.results[0]["out_0_dram"]
```

```python
from contextlib import ExitStack

import concourse.bass as bass
from concourse import mybir

F32 = mybir.dt.float32
F32R = mybir.dt.float32r
BF16 = mybir.dt.bfloat16
I32 = mybir.dt.int32
ALU = mybir.AluOpType
ACT = mybir.ActivationFunctionType
AX = mybir.AxisListType.X

P = 128
S = 256
T = S // P
D = 1024
KC = D // P
FF = 2816
FC = FF // P
HALF = 256
UPB = FF // HALF
UNIT = 1024
RAW = 8
SPLIT = 4
EPS = 1e-6
NEG = -1e30
TAPS = 31
NH = 16
HD = 64
GH = 4
GDK = 128
GDV = 256
LEVELS = [64, 32, 16, 8, 4, 2, 1]
AUG = HD + 2

ROWS = ([("dw_w", i) for i in range(TAPS)] + [("dw_b", 0), ("conv_ln_g", 0), ("conv_ln_b", 0),
        ("mix_norm", 0), ("ffn2_norm", 0), ("ple_gate_norm", 0), ("g_pre_2", 0), ("g_pre_2", 1), ("g_pre_2", 2),
        ("c_2", 0)] + [("b_ada_2", m) for m in (0, 1, 3, 4, 6, 7)])
ROW = {}
for _i, (_n, _k) in enumerate(ROWS):
    ROW[(_n, _k)] = _i
NROW = len(ROWS)

C_ID, C_ONES, C_TRI, C_D, C_W, C_COS, C_SIN, C_GLA = 0, 128, 256, 384, 512, 640, 656, 672
NGLA = 1 + len(LEVELS)
NCONST = C_GLA + NGLA * P


def shape_constants():
    import numpy as np

    t = np.zeros((P, NCONST), np.float32)
    i = np.arange(P)
    t[:, C_ID:C_ID + P] = np.eye(P)
    t[:, C_ONES:C_ONES + P] = 1.0
    t[:, C_TRI:C_TRI + P] = i[:, None] <= i[None, :]
    t[:, C_D:C_D + P] = np.where(i[None, :] <= i[:, None], 0.0, NEG)
    t[:, C_W:C_W + P] = np.where(i[None, :] > i[:, None], 0.0, NEG)
    inv = np.float32(500000.0) ** (-np.arange(0, 16, 2, dtype=np.float32) / np.float32(16))
    ang = np.arange(S, dtype=np.float32)[:, None] * inv[None, :].astype(np.float32)
    for n in range(T):
        t[:, C_COS + 8 * n:C_COS + 8 * n + 8] = np.cos(ang[n * P:(n + 1) * P])
        t[:, C_SIN + 8 * n:C_SIN + 8 * n + 8] = np.sin(ang[n * P:(n + 1) * P])
    s, q = i[:, None], i[None, :]
    t[:, C_GLA:C_GLA + P] = s == q
    for n, L in enumerate(LEVELS):
        pair = (s // (2 * L) == q // (2 * L)) & (s // L % 2 == 0) & (q // L % 2 == 1)
        t[:, C_GLA + (n + 1) * P:C_GLA + (n + 2) * P] = pair
    return t


def two_blocks(nc, A, consts, out):
    ctx = ExitStack()
    with ctx:
        at = [nc.sbuf_base + 31 & ~31]

        def place(name, shape, dt=F32, base=None):
            size = 1
            for n in shape[1:]:
                size *= n
            size *= 2 if dt == BF16 else 4
            if base is None:
                base = at[0]
                at[0] += size + 31 & ~31
            return nc.alloc_sbuf_tensor_at(name, shape, dt, offset=base), base, base + (size + 31 & ~31)

        def keep(name, shape, dt=F32):
            return place(name, shape, dt)[0]

        raw = keep("raw", [P, RAW, UNIT])
        w_hi = keep("w_hi", [P, SPLIT, UNIT], F32R)
        w_lo = keep("w_lo", [P, SPLIT, UNIT], F32R)
        x = keep("x", [P, T, D])
        a_hi = keep("a_hi", [P, KC, S], F32R)
        a_lo = keep("a_lo", [P, KC, S], F32R)
        b_hi, B0, _ = place("b_hi", [P, KC, S], F32R)
        b_lo = keep("b_lo", [P, KC, S], F32R)
        GT, GT0, _ = place("GT", [P, 3, D])
        const = keep("const", [P, C_GLA])
        identb = keep("identb", [P, P], BF16)
        maskD = keep("maskD", [P, P], BF16)
        maskWD = keep("maskWD", [P, 2 * P], BF16)
        par = keep("par", [P, KC, NROW])
        csil = keep("csil", [P, KC])
        gain0 = keep("gain0", [P, KC])
        modA = keep("modA", [P, 3, KC])
        modB = keep("modB", [P, 3, KC])
        gq = keep("gq", [P, HD])
        gk = keep("gk", [P, HD])
        sinkb = keep("sinkb", [P, NH])
        bfb = keep("bfb", [P, NH])
        baT = keep("baT", [P, GH])
        wa2 = keep("wa2", [16, 512])
        ss = keep("ss", [P, 2])
        rstd = keep("rstd", [P, 2])
        pss = keep("pss", [P, 2])
        prs = keep("prs", [P, 2])
        rt = keep("rt", [P, 3, 36])
        rs36 = keep("rs36", [P, 36])
        st = keep("st", [P, 2, 6, 4])
        kd, KD0, _ = place("kd", [P, GH * S])
        b_lo_f, _, _ = place("b_lo_f", [P, 2 * S], F32, KD0)
        prod, _, _ = place("prod", [P, 4, S], F32, KD0)
        ARENA2 = at[0]
        ada = keep("ada", [P, 3, D])
        acc_m = keep("acc_m", [P, 2, D])
        brow = keep("brow", [3, D])
        ARENA = at[0]
        hid_hi, _, e = place("hid_hi", [P, FC, S], F32R, ARENA)
        hid_lo, _, e = place("hid_lo", [P, FC, S], F32R, e)
        HB = e
        h, _, _ = place("h", [P, T, D], F32, HB)
        sg, _, e = place("sg", [P, 2, T, HALF], F32, HB)
        hid, _, END = place("hid", [P, 2, T, HALF], F32, e)
        assert END <= nc.sbuf_usable_end, (END, nc.sbuf_usable_end)
        prow, _, _ = place("prow", [NROW, D], F32, ARENA)
        csg, _, e = place("csg", [P, 2, T, HALF], F32, ARENA)
        cub, _, e = place("cub", [P, 2, T, HALF], F32, e)
        uT, _, e = place("uT", [P, KC, S + TAPS - 1], F32, e)
        y, _, e = place("y", [P, KC, S], F32, e)
        qkv, Q0, e = place("qkv", [P, T, 1280], F32, e)
        gates, _, e = place("gates", [P, T, 2 * D], F32, e)
        assert e <= END, (e, END)
        qT, _, _ = place("qT", [P, KC, S], F32, ARENA)
        cf, _, _ = place("cf", [P, KC, S], F32, ARENA)
        ysq, _, e = place("ysq", [P, KC, S], F32, Q0)
        lnb, _, e = place("lnb", [P, 2, S], F32, e)
        lnt, _, _ = place("lnt", [P, 3, S], F32, B0)
        qsq, _, e = place("qsq", [P, T, 18, HD], F32, B0)
        rope, _, e = place("rope", [P, T, 4, 18, 8], F32, e)
        assert e <= GT0
        pr, _, e = place("pr", [P, 2, 512], F32, B0)
        pt, _, e = place("pt", [P, 2, 512], F32, e)
        kTz, _, e = place("kTz", [P, 2, 2, S], F32, e)
        kdup, _, e = place("kdup", [P, T, 2, 2, HD], F32, e)
        assert e <= GT0
        emb, _, e = place("emb", [P, T, D], F32, ARENA)
        grow, _, _ = place("grow", [P, D], F32, B0 + 4096)
        pin, _, _ = place("pin", [P, T, 256], F32, B0 + 12288)
        va, _, e = place("va", [P, T, D], F32, ARENA2)
        ra, _, e = place("ra", [P, T, D], F32, e)
        gates2, _, _ = place("gates2", [P, T, 2 * D], F32, ARENA2)
        qa, QA0, e = place("qa", [P, GH, S], F32, e)
        ka, _, e = place("ka", [P, GH, S], F32, e)
        ggla, _, e = place("ggla", [P, D], F32, e)
        bc, _, e = place("bc", [P, GH, S], F32, e)
        AT, _, e = place("AT", [P, 3, GH, P], F32, e)
        qb, _, e = place("qb", [AUG, NH, S], F32, e)
        kb, _, e = place("kb", [AUG, NH, S], F32, e)
        vb, _, e = place("vb", [P, T, D], F32, e)
        ga_ss, _, e = place("ga_ss", [P, 5, 8], F32, e)
        assert e <= nc.sbuf_usable_end
        glam, _, _ = place("glam", [P, NGLA, P], F32, GT0)
        zt, _, _ = place("zt", [P, T, 512], F32, B0)
        aug, _, e = place("aug", [P, T, 8, AUG], F32, B0)
        AUGB = e - B0
        ya, _, e = place("ya", [P, GH, S], F32, e)
        la, _, e = place("la", [P, GH, S], F32, e)
        assert e <= GT0
        dd, _, e = place("dd", [P, 2, 512], F32, B0 + AUGB)
        gtmp, _, e = place("gtmp", [P, 512], F32, e)
        qd, _, e = place("qd", [P, GH * S], F32, e)
        sm, _, e = place("sm", [P, T, 32], F32, e)
        lf, _, e = place("lf", [P, 3, T, NH], F32, e)
        Fc, _, e = place("Fc", [P, T, NH], F32, e)
        alT, _, e = place("alT", [16, S], F32, e)
        assert e <= GT0
        pr2, _, e = place("pr2", [P, 2, 512], F32, QA0)
        pt2, _, e = place("pt2", [P, 2, 512], F32, e)

        ps = ctx.enter_context(nc.psum_tensor("ps", [P, 8, 512], F32))

        def acc(t, s):
            return ps[:, 2 * t + s, :]

        def wide(t):
            return ps[:, 2 * t:2 * t + 2, :].rearrange("p b n -> p (b n)")

        def behind(t):
            return ps[:, 4 + 2 * t:6 + 2 * t, :].rearrange("p b n -> p (b n)")

        ident = const[:, C_ID:C_ID + P]
        ones = const[:, C_ONES:C_ONES + P]

        sems = {}

        def sem(name):
            if name not in sems:
                sems[name] = ctx.enter_context(nc.semaphore(name))
            return sems[name]

        units = []

        def cols_units(W, c0, n, c1=None):
            v = W.rearrange("(c p) n -> p c n", p=P)
            first = len(units)
            for i in range(0, KC, 2):
                if c1 is None:
                    units.append(([v[:, i:i + 2, c0:c0 + n]], 2, n))
                else:
                    units.append(([v[:, i:i + 2, c0:c0 + n // 2], v[:, i:i + 2, c1:c1 + n // 2]], 2, n))
            return first

        def row_units(W):
            v = W.rearrange("(c p) n -> p c n", p=P)
            first = len(units)
            for i in range(W.shape[0] // P):
                units.append(([v[:, i:i + 1, :]], 1, D))
            return first

        def ffn_units(wgu, wdn):
            up = [cols_units(wgu, j * HALF, 2 * HALF, FF + j * HALF) for j in range(UPB)]
            return up[0], row_units(wdn)

        ffn = [None] * 4
        ffn[0] = ffn_units(A["ffn1_wgu"][0], A["ffn1_wdown"][0])
        w_in = A["w_in"][0]
        CA, CB, ZG = 1280, 2304, 3328
        u_mix = [cols_units(w_in, CA + j * HALF, 512, CB + j * HALF) for j in range(4)]
        u_mix += [cols_units(w_in, 0, 512), cols_units(w_in, 512, 512), cols_units(w_in, 1024, 256)]
        u_mix += [cols_units(w_in, ZG + 512 * i, 512) for i in range(4)]
        u_ap = row_units(A["attn_proj"][0])
        u_cp = row_units(A["conv_proj"][0])
        u_wo = row_units(A["w_out"][0])
        ffn[1] = ffn_units(A["ffn2_wgu"][0], A["ffn2_wdown"][0])
        u_pp = row_units(A["ple_proj"][0])
        u_pg = row_units(A["ple_gate_w"][0])
        ffn[2] = ffn_units(A["w_gu1_2"][0], A["w_dn1_2"][0])
        w_in2 = A["w_in_2"][0]
        M2 = len(units)
        v = w_in2.rearrange("(c p) n -> p c n", p=P)
        units.append(([v[:, :, 2048:2064], v[:, :, 6160:6176]], KC, 32))
        c2 = [0, 512, 1024, 1536, 2064, 2576, 3088, 3600, 4112, 4624, 5136, 5648, 6176, 6688, 7200, 7712]
        u_mix2 = [M2] + [cols_units(w_in2, c, 512) for c in c2]
        u_pa = row_units(A["w_pa_2"][0])
        u_pb = row_units(A["w_pb_2"][0])
        u_wo2 = row_units(A["w_out_2"][0])
        ffn[3] = ffn_units(A["w_gu2_2"][0], A["w_dn2_2"][0])
        NU = len(units)

        count = [0] * RAW
        need = []
        for u in range(NU):
            count[u % RAW] += 16 * len(units[u][0])
            need.append(count[u % RAW])

        landed = [sem(f"raw_landed{r}") for r in range(RAW)]
        hi_ready, lo_ready, used = sem("w_hi_ready"), sem("w_lo_ready"), sem("unit_used")

        class Stream:

            def __init__(self, part):
                self.part, self.at = part, 0

            def to(self, n):
                while self.at < min(n, NU):
                    self.part(self.at)
                    self.at += 1

        NORM = {"f0": 0, "mix": 1, "f1": 2, "gate": 3, "f2": 4, "mix2": 5, "f3": 6}
        TURN = {"f0": 0, "mix": 1, "merge": 2, "f1": 3, "gate": 4, "f2": 5, "mix2": 6, "oa": 7, "merge2": 8, "f3": 9}
        ONE_ROW = ["dw_b", "conv_ln_g", "conv_ln_b", "mix_norm", "ffn2_norm", "ple_gate_norm", "c_2"]
        MADE = {"merge": 0, "f2": 1, "mix2": 2, "oa": 3, "merge2": 4, "f3": 5}
        FOLDED = ["f0", "mix", "f1", "gate"]
        SCALE_ROW = {"mix": ("mix_norm", 0), "f1": ("ffn2_norm", 0), "gate": ("ple_gate_norm", 0)}

        def gain(key, c):
            if key == "f0":
                return gain0[:, c:c + 1]
            r = ROW[SCALE_ROW[key]]
            return par[:, c, r:r + 1]

        MODS = {"f2": 0, "mix2": 1, "f3": 2}
        FFN = ["f0", "f1", "f2", "f3"]
        POST = {"emb": 0, "f2": 1, "mix2": 2, "f3": 3}

        POOLC = 4
        VC = KC - POOLC
        CONV_AT, CONV_G = [0, 16, 32, 32, 38, 44, 60], 5
        PROD_U, PROD_G = 3, 4
        ADA_F = 24
        MOD_AT = {}
        for f in range(3):
            MOD_AT.update({(f"f{f}", 5): (3 * f,), (f"f{f}", 9): (3 * f + 1,), (f"f{f}", UPB + 1): (3 * f + 2,)})
        TURN_BANKS = [4, 6, 5, 7]
        NSTEP = 2 + len(LEVELS)

        block = ctx.enter_context(nc.Block())

        GROUPS = [(0, 4 * i, 4, 1) for i in range(4)] + [(1, 2 * i, 2, 2) for i in range(8)]
        NG = len(GROUPS)

        def exps(m, i):
            n = (NG + sum(g[2] for g in GROUPS)) * m
            return n + sum(g[2] + (m == 0) for g in GROUPS[:i + 1])

        ENDS = {1: (0, 0), 3: (0, 1), 7: (1, 0), 11: (1, 1)}

        @block.sync
        def _(sp):
            def load_unit(u):
                src, nk, n = units[u]
                if u >= RAW:
                    sp.wait_ge(lo_ready, u - RAW + 1)
                dst = raw[:, u % RAW, 0:nk * n].rearrange("p (c n) -> p c n", c=nk)
                if len(src) == 1:
                    sp.dma_start(dst, src[0]).then_inc(landed[u % RAW], 16)
                else:
                    sp.dma_start(dst[:, :, 0:n // 2], src[0]).then_inc(landed[u % RAW], 16)
                    sp.dma_start(dst[:, :, n // 2:n], src[1]).then_inc(landed[u % RAW], 16)

            sp.dma_start(x[:, :, :], A["x"][0].rearrange("(t p) d -> p t d", p=P)).then_inc(sem("x_landed"), 16)
            for u in range(NU):
                load_unit(u)
            for t in range(T):
                sp.wait_ge(sem("x_ready"), 24 + 2 * (t + 1))
                sp.dma_start(out[0, t * P:(t + 1) * P, :], x[:, t, :]).then_inc(sem("out_stored"), 16)
            sp.wait_ge(sem("out_stored"), 16 * T)

        @block.gpsimd
        def _(pool):
            w_ada = A["w_ada_2"][0].rearrange("(c p) n -> c p n", p=P)

            def load_ada(i0, i1):
                for i in range(i0, i1):
                    m, k = i // KC, i % KC
                    if i >= 3:
                        pool.wait_ge(sem("ada_used"), i - 2)
                    pool.dma_start(ada[:, i % 3, :], w_ada[k, :, m * D:(m + 1) * D]).then_inc(sem(f"ada_landed{i % 3}"), 16)

            v = A["b_ada_2"][0].rearrange("(g k d) -> g k d", g=3, k=3)
            rows = [(("dw_w", 0), TAPS, A["dw_w"][0]), (("g_pre_2", 0), 3, A["g_pre_2"][0])]
            rows += [(("b_ada_2", 3 * g), 2, v[g, 0:2, :]) for g in range(3)]
            rows += [((n, 0), 1, A[n][0:1, :]) for n in ONE_ROW]
            for key, n, src in rows:
                i = ROW[key]
                pool.dma_start(prow[i:i + n, :], src).then_inc(sem("prow_landed"), 16)
            for dst, src in ((gq, "q_norm"), (gk, "k_norm"), (sinkb, "sinks"), (bfb, "b_f_2")):
                pool.dma_start(dst[:, :], A[src][0].partition_broadcast(P)).then_inc(sem("small_landed"), 16)
            pool.dma_start(baT[:, :], A["b_a_2"][0].rearrange("(h p) -> p h", p=P), allow_slow_non_contiguous=True)\
                .then_inc(sem("small_landed"), 16)
            pool.dma_start(wa2[:, :], A["w_a2_2"][0]).then_inc(sem("small_landed"), 16)
            pool.wait_ge(used, 2)
            load_ada(0, 3)
            for g in range(3):
                pool.dma_start(GT[:, g, :], A["g_post_2"][0, g].partition_broadcast(P)).then_inc(sem("gpost_landed"), 16)
                m = 3 * g + 2
                pool.dma_start(brow[g:g + 1, :], A["b_ada_2"][0:1, m * D:(m + 1) * D]).then_inc(sem("gpost_landed"), 16)
            load_ada(3, ADA_F + 3)
            for i in range((TAPS - 1) * POOLC):
                c = VC + i % POOLC
                pool.wait_ge(sem("conv_product"), POOLC + i + 1)
                if i >= POOLC:
                    pool.wait_ge(sem("pool_step"), i - POOLC + 1)
                pool.tensor_tensor(y[:, c, :], y[:, c, :], prod[:, i % 4, :], ALU.add).then_inc(sem("pool_step"), 1)
            load_ada(ADA_F + 3, ADA_F + 9)
            pool.wait_ge(used, u_wo)
            pool.dma_start(pin[:, :, :], A["p"][0, 0].rearrange("(t p) d -> p t d", p=P)).then_inc(sem("pin_landed"), 16)
            pool.dma_start(grow[:, :], A["ple_norm"][0].partition_broadcast(P)).then_inc(sem("grow_landed"), 16)
            load_ada(ADA_F + 9, 3 * ADA_F)
            pool.wait_ge(sem("x_ready"), 20)
            pool.dma_start(glam[:, :, :], consts[:, C_GLA:NCONST].rearrange("p (m n) -> p m n", n=P)).then_inc(sem("glam_landed"), 16)
            pool.dma_start(ggla[:, :], A["g_gla_2"][0].partition_broadcast(P)).then_inc(sem("glam_landed"), 16)

        @block.scalar
        def _(act):
            def hi_part(u):
                _, nk, n = units[u]
                act.wait_ge(landed[u % RAW], need[u])
                if u >= SPLIT:
                    act.wait_ge(used, u - SPLIT + 1)
                act.activation(w_hi[:, u % SPLIT, 0:nk * n], raw[:, u % RAW, 0:nk * n], ACT.Copy).then_inc(hi_ready, 1)

            w = Stream(hi_part)

            def norm_squares(key, junk):
                q = NORM[key]
                for t in range(T):
                    if q == 0:
                        act.wait_ge(sem("x_landed"), 16)
                    else:
                        act.wait_ge(sem("x_ready"), 4 * q if key in FOLDED else 4 * q - 2 + 2 * t)
                    if TURN[key] > 0:
                        act.wait_ge(sem("turned"), 4 * TURN[key])
                    act.activation(junk[:, t, :], x[:, t, :], ACT.Square, accum_out=ss[:, t:t + 1]).then_inc(sem("ss_ready"), 1)

            def turned_hi(key, hi=a_hi):
                k = TURN[key]
                for c in range(KC):
                    if c % 2 == 0:
                        act.wait_ge(sem("turned"), 4 * k + c // 2 + 1)
                    src = ps[:, TURN_BANKS[c // 2], (c % 2) * S:(c % 2 + 1) * S]
                    if key in FOLDED:
                        i = act.activation(hi[:, c, :], src, ACT.Copy, scale=gain(key, c))
                    elif key in MODS:
                        g = MODS[key]
                        i = act.activation(hi[:, c, :], src, ACT.Identity, scale=modA[:, g, c:c + 1], bias=modB[:, g, c:c + 1])
                    else:
                        i = act.activation(hi[:, c, :], src, ACT.Copy)
                    i.then_inc(sem("act_hi"), 1)

            def post_squares(key, junk, end=None):
                for t in range(T):
                    if end is not None and t == 0:
                        act.wait_ge(sem("first_tile"), POST[key] + 1)
                    elif end is not None:
                        act.wait_ge(used, end)
                    act.activation(junk[:, t, :], wide(t), ACT.Square, accum_out=pss[:, t:t + 1]).then_inc(sem("pss_ready"), 1)

            def ffn_part(f):
                up, dn = ffn[f]
                for j in range(UPB):
                    w.to(up + 4 * j + 6)
                    if j == 0 and f < 2:
                        act.wait_ge(sem("rstd_ready"), NORM[FFN[f]] + 1)
                    if j == 0 and f == 0:
                        act.wait_ge(sem("par_ready"), 1)
                        act.activation(csil[:, :], par[:, :, ROW[("c_2", 0)]], ACT.Silu).then_inc(sem("csil_ready"), 1)
                    if j >= 1:
                        hidden_hi(f, j - 1)
                    w.to(up + 4 * j + 8)
                    act.wait_ge(used, up + 4 * j + 4)
                    for t in range(T):
                        if j >= 2:
                            act.wait_ge(sem("hid_ready"), f * UPB + j - 1)
                        act.activation(sg[:, j % 2, t, :], acc(t, j % 2)[:, 0:HALF], ACT.Silu,
                                       scale=rstd[:, t:t + 1] if f < 2 else 1.0).then_inc(sem("silu_ready"), 1)
                w.to(dn + 5)
                hidden_hi(f, UPB - 1)
                w.to(dn + FC + 3)

            def hidden_hi(f, j):
                act.wait_ge(sem("hid_turned"), f * UPB + j + 1)
                act.activation(hid_hi[:, 2 * j:2 * j + 2, :].rearrange("p c n -> p (c n)"), ps[:, 4 + j % 2, :], ACT.Copy)\
                   .then_inc(sem("hid_hi_ready"), 1)

            def attention_part(m):
                prb, ptb = (pr, pt) if m == 0 else (pr2, pt2)
                g0, e0 = NG * m, 4 * m
                for i in range(NG + 3):
                    if i < NG:
                        n, h0, nh, nk = GROUPS[i]
                        act.wait_ge(sem("bias_ready"), g0 + i + 1)
                        if i >= 2:
                            act.wait_ge(sem("probs_turned"), g0 + i - 1)
                        L = nk * P
                        for q in range(nh):
                            act.activation(prb[:, i % 2, q * L:(q + 1) * L], ps[:, 4 + i % 4, q * L:(q + 1) * L], ACT.Exp,
                                           bias=st[:, i % 2, 1, q:q + 1], scale=HD ** -0.5 if m == 0 else 1.0,
                                           accum_out=st[:, i % 2, 2, q:q + 1]).then_inc(sem("exp_done"), 1)
                        if m == 0:
                            products(24 * PROD_U + i * PROD_G, 24 * PROD_U + (i + 1) * PROD_G)
                            act.activation(st[:, i % 2, 3, 0:nh], st[:, i % 2, 4, 0:nh], ACT.Exp).then_inc(sem("exp_done"), 1)
                    if 2 <= i < NG + 2:
                        act.wait_ge(sem("probs_turned"), g0 + i - 1)
                        if i >= 4:
                            act.wait_ge(sem("values_done"), g0 + i - 3)
                        act.activation(ptb[:, i % 2, :], ps[:, i % 2, :], ACT.Copy).then_inc(sem("pt_ready"), 1)
                    if m == 0 and i >= NG:
                        products(24 * PROD_U + i * PROD_G, 24 * PROD_U + (i + 1) * PROD_G)
                    if i - 3 in ENDS:
                        n, g = ENDS[i - 3]
                        act.wait_ge(sem("values_done"), g0 + i - 2)
                        act.activation(a_hi[:, 4 * g:4 * g + 4, n * P:(n + 1) * P], ps[:, 2 + g, :].rearrange("p (c q) -> p c q", q=P),
                                       ACT.Copy).then_inc(sem("att_hi"), 1)

            def folded_norm(key):
                turned_hi(key)
                norm_squares(key, h)

            def products(i0, i1):
                for i in range(i0, min(i1, TAPS * POOLC)):
                    k, c = i // POOLC, VC + i % POOLC
                    src = uT[:, c, k:k + S]
                    if i == 0:
                        act.wait_ge(sem("uT_ready"), 5)
                    if k == 0:
                        r = ROW[("dw_b", 0)]
                        ins = act.activation(y[:, c, :], src, ACT.Identity, scale=par[:, c, 0:1], bias=par[:, c, r:r + 1])
                    else:
                        j = i - POOLC
                        if j >= 4:
                            act.wait_ge(sem("pool_step"), j - 3)
                        ins = act.activation(prod[:, j % 4, :], src, ACT.Copy, scale=par[:, c, k:k + 1])
                    ins.then_inc(sem("conv_product"), 1)

            act.dma_start(const[:, :], consts[:, 0:C_GLA]).then_inc(sem("const_landed"), 16)
            act.dma_start(gain0[:, :], A["ffn1_norm"][0].rearrange("(c p) -> p c", p=P), allow_slow_non_contiguous=True)\
               .then_inc(sem("gain0_landed"), 16)
            act.wait_ge(sem("gain0_landed"), 16)
            turned_hi("f0")
            w.to(4)
            norm_squares("f0", h)
            ffn_part(0)
            w.to(ffn[0][1] + FC + 4)
            folded_norm("mix")

            M = u_mix[0]
            for b in range(11):
                n = 4 * PROD_U * (b - 5)
                w.to(M + 4 * b + 5)
                if b >= 5:
                    products(n, n + PROD_U)
                w.to(M + 4 * b + 6)
                if b >= 5:
                    products(n + PROD_U, n + 2 * PROD_U)
                if b == 10:
                    for c in range(4):
                        act.wait_ge(sem("q_turned"), c + 1)
                        act.activation(qT[:, 2 * c:2 * c + 2, :].rearrange("p c n -> p (c n)"), ps[:, 4 + c, :], ACT.Copy)\
                           .then_inc(sem("qT_ready"), 1)
                if 1 <= b <= 4:
                    act.wait_ge(sem("conv_turned"), b)
                    j = b - 1
                    act.activation(uT[:, 2 * j:2 * j + 2, TAPS - 1:], ps[:, 4 + j % 2, :].rearrange("p (c n) -> p c n", c=2),
                                   ACT.Copy).then_inc(sem("uT_ready"), 1)
                w.to(M + 4 * b + 7)
                if b >= 5:
                    products(n + 2 * PROD_U, n + 3 * PROD_U)
                w.to(M + 4 * b + 8)
                act.wait_ge(used, M + 4 * b + 4)
                if b >= 5:
                    products(n + 3 * PROD_U, n + 4 * PROD_U)
                if b == 0:
                    act.wait_ge(sem("rstd_ready"), NORM["mix"] + 1)
                for t in range(T):
                    r = rstd[:, t:t + 1]
                    if b < 4:
                        if b >= 2:
                            act.wait_ge(sem("cub_ready"), b - 1)
                        act.activation(csg[:, b % 2, t, :], acc(t, b % 2)[:, HALF:], ACT.Sigmoid, scale=r).then_inc(sem("csg_ready"), 1)
                    elif b < 7:
                        c0 = 512 * (b - 4)
                        n = 512 if b < 6 else 256
                        act.activation(qkv[:, t, c0:c0 + n], acc(t, b % 2)[:, 0:n], ACT.Copy, scale=r).then_inc(sem("mix_evac"), 1)
                    else:
                        c0 = 512 * (b - 7)
                        act.activation(gates[:, t, c0:c0 + 512], acc(t, b % 2), ACT.Sigmoid, scale=r).then_inc(sem("mix_evac"), 1)
            attention_part(0)
            w.to(u_ap + 5)
            act.wait_ge(sem("yc_ready"), 1)
            act.activation(ysq[:, :, :], y[:, :, :], ACT.Square).then_inc(sem("ysq_ready"), 1)
            w.to(u_cp + 2)
            act.wait_ge(sem("yn_ready"), 1)
            for c in range(KC):
                g, b = ROW[("conv_ln_g", 0)], ROW[("conv_ln_b", 0)]
                act.activation(cf[:, c, :], y[:, c, :], ACT.Silu, scale=par[:, c, g:g + 1], bias=par[:, c, b:b + 1]).then_inc(sem("cf_ready"), 1)
                if c % 2 == 1:
                    act.wait_ge(sem("cf_ready"), c + 1)
                    act.activation(b_hi[:, c - 1:c + 1, :], cf[:, c - 1:c + 1, :], ACT.Copy).then_inc(sem("b_hi_ready"), 1)
            w.to(u_wo + 4)
            turned_hi("merge")
            w.to(ffn[1][0] + 4)
            folded_norm("f1")
            ffn_part(1)
            act.wait_ge(sem("pin_turned"), 1)
            act.activation(b_hi[:, 0:2, :].rearrange("p c n -> p (c n)"), ps[:, 4, :], ACT.Copy).then_inc(sem("pin_hi"), 1)
            w.to(u_pp + 4)
            turned_hi("gate")
            w.to(u_pg + 4)
            norm_squares("gate", h)
            w.to(u_pg + 6)
            post_squares("emb", emb)
            w.to(u_pg + KC + 3)
            act.wait_ge(sem("rstd_ready"), NORM["gate"] + 1)
            for t in range(T):
                if t == 0:
                    act.wait_ge(sem("first_tile"), 1)
                else:
                    act.wait_ge(used, u_pg + KC)
                act.activation(h[:, t, :], behind(t), ACT.Sigmoid, scale=rstd[:, t:t + 1]).then_inc(sem("gate_ready"), 1)
            w.to(u_pg + KC + 4)
            norm_squares("f2", h)
            turned_hi("f2")
            ffn_part(2)
            post_squares("f2", h, ffn[2][1] + FC)
            w.to(ffn[2][1] + FC + 4)
            norm_squares("mix2", h)
            turned_hi("mix2")

            def between(b):
                if b == 1:
                    act.wait_ge(sem("alow_turned"), 1)
                    act.activation(alT[:, :], ps[0:16, 6, 0:S], ACT.Copy).then_inc(sem("alT_ready"), 1)
                    act.wait_ge(sem("nf_ready"), 1)
                    act.activation(lf[:, 1, :, :], lf[:, 1, :, :], ACT.Exp).then_inc(sem("act_step"), 1)
                    act.wait_ge(sem("act_step"), 1)
                    act.activation(lf[:, 1, :, :], lf[:, 1, :, :], ACT.Ln, bias=1.0).then_inc(sem("lnf_ready"), 1)
                if b in (2, 3):
                    act.wait_ge(sem("z_turned"), b - 1)
                    dst = (qa if b == 2 else ka)[:, :, :].rearrange("p h n -> p (h n)")
                    act.activation(dst, ps[:, 4:6, :].rearrange("p b n -> p (b n)"), ACT.Copy).then_inc(sem("qka_ready"), 1)
                if b == 3:
                    act.wait_ge(sem("na_ready"), 1)
                    act.activation(la[:, :, :], la[:, :, :], ACT.Exp).then_inc(sem("act_step"), 1)
                    act.wait_ge(sem("act_step"), 2)
                    act.activation(la[:, :, :], la[:, :, :], ACT.Ln, bias=1.0).then_inc(sem("lna_ready"), 1)
                if 8 <= b <= 11:
                    act.wait_ge(sem("z_turned"), b - 5)
                    dst = qb if b < 10 else kb
                    for i in range(2):
                        h0 = 8 * (b % 2) + 2 * i
                        act.activation(dst[:, h0:h0 + 2, :].rearrange("p h n -> p (h n)"), ps[0:AUG, 4 + i, :], ACT.Copy)\
                           .then_inc(sem("qkb_act"), 1)

            w.to(M2 + 4)
            for b in range(13):
                u1 = u_mix2[b + 1]
                if b >= 5:
                    w.to(u1 + 1)
                    act.wait_ge(sem("diff_ready"), b - 4)
                    act.activation(dd[:, :, :], dd[:, :, :], ACT.Exp, scale=1.0 / 16.0).then_inc(sem("decay_ready"), 1)
                w.to(u1 + 2)
                between(b)
                w.to(u1 + 4)
                act.wait_ge(used, u1)
                for t in range(T):
                    src = acc(t, b % 2)
                    if b == 0:
                        i = act.activation(sm[:, t, :], src[:, 0:32], ACT.Copy)
                    elif b in (1, 2):
                        if b == 2:
                            act.wait_ge(sem("z_turned"), 1)
                        i = act.activation(zt[:, t, :], src, ACT.Copy, scale=GDK ** -0.5 if b == 1 else 1.0)
                    elif b in (3, 4):
                        i = act.activation(va[:, t, 512 * (b - 3):512 * (b - 2)], src, ACT.Copy)
                    elif b in (5, 6):
                        i = act.activation(ra[:, t, 512 * (b - 5):512 * (b - 4)], src, ACT.Silu)
                    elif b in (7, 8, 9, 10):
                        act.wait_ge(sem("z_turned"), b - 5)
                        i = act.activation(aug[:, t, :, 0:HD], src.rearrange("p (h d) -> p h d", d=HD), ACT.Copy,
                                           scale=HD ** -0.5 if b < 9 else 1.0)
                    else:
                        i = act.activation(vb[:, t, 512 * (b - 11):512 * (b - 10)], src, ACT.Copy)
                    i.then_inc(sem("mix2_evac"), 1)

            for t in range(T):
                act.wait_ge(sem("gla_out"), t + 1)
                for q in range(GH):
                    act.activation((qd, kd)[t][:, q * GDV:(q + 1) * GDV], ps[:, 4 + 2 * t + q // 2, (q % 2) * GDV:(q % 2 + 1) * GDV],
                                   ACT.Square, accum_out=ga_ss[:, 0, t * GH + q:t * GH + q + 1]).then_inc(sem("gla_squares"), 1)
            G = u_mix2[13]
            for b in range(4):
                w.to(G + 4 * b + 8)
                if b == 0:
                    continue
                if b == 1:
                    turned_hi("oa", b_hi)
                for e in ((0, 1) if b == 1 else (b,)):
                    act.wait_ge(used, G + 4 * e + 4)
                    for t in range(T):
                        act.activation(gates2[:, t, 512 * e:512 * e + 512], acc(t, e % 2), ACT.Sigmoid).then_inc(sem("gates2_ready"), 1)
            attention_part(1)
            w.to(u_wo2 + 4)
            turned_hi("merge2")
            w.to(u_wo2 + KC + 3)
            post_squares("mix2", h, u_wo2 + KC)
            w.to(u_wo2 + KC + 4)
            norm_squares("f3", h)
            turned_hi("f3")
            ffn_part(3)
            post_squares("f3", h, ffn[3][1] + FC)

        @block.vector
        def _(dve):
            def lo_part(u):
                _, nk, n = units[u]
                dve.wait_ge(hi_ready, u + 1)
                dve.tensor_tensor(w_lo[:, u % SPLIT, 0:nk * n], raw[:, u % RAW, 0:nk * n],
                                  w_hi[:, u % SPLIT, 0:nk * n].bitcast(F32), ALU.subtract).then_inc(lo_ready, 1)

            w = Stream(lo_part)
            steps = [0]

            def then(ins):
                steps[0] += 1
                ins.then_inc(sem("dve_step"), 1)
                dve.wait_ge(sem("dve_step"), steps[0])

            def rsqrt(dst, src, scale, tmp, signal=None, count=0):
                v, a = tmp[0], tmp[1]
                then(dve.tensor_scalar(v, src, scale, EPS, ALU.mult, ALU.add))
                then(dve.tensor_scalar(a.bitcast(I32), v.bitcast(I32), 1, None, ALU.logical_shift_right))
                then(dve.tensor_scalar(dst.bitcast(I32), a.bitcast(I32), -1.0, 1597463007.0, ALU.mult, ALU.add))
                for n in range(3):
                    then(dve.tensor_tensor(a, dst, dst, ALU.mult))
                    then(dve.scalar_tensor_tensor(a, a, -0.5, v, ALU.mult, ALU.mult))
                    i = dve.scalar_tensor_tensor(dst, a, 1.5, dst, ALU.add, ALU.mult)
                    if n == 2 and signal is not None:
                        i.then_inc(signal, 1)
                        dve.wait_ge(signal, count)
                    else:
                        then(i)

            def small(r, n=2):
                return [rt[:, 0, 0:n], rt[:, 1, 0:n]]

            def normalise(key):
                row_scales(key)
                for n in range(2):
                    for t in range(T):
                        c = slice(512 * n, 512 * (n + 1))
                        dve.tensor_scalar(h[:, t, c], x[:, t, c], rstd[:, t:t + 1], None, ALU.mult).then_inc(sem("h_ready"), 1)

            def folded_norm(key):
                turned_lo(key)
                row_scales(key)

            def row_scales(key):
                q = NORM[key]
                dve.wait_ge(sem("ss_ready"), 2 * q + 2)
                rsqrt(rstd[:, :], ss[:, :], 1.0 / D, small(rt), sem("rstd_ready"), q + 1)

            def add_to_x(key, factor):
                for n in range(2):
                    for t in range(T):
                        c = slice(512 * n, 512 * (n + 1))
                        dve.scalar_tensor_tensor(x[:, t, c], acc(t, n), factor, x[:, t, c], ALU.mult, ALU.add).then_inc(sem("x_ready"), 1)

            def turned_lo(key, hi=a_hi, lo=a_lo):
                k = TURN[key]
                for c in range(KC):
                    dve.wait_ge(sem("act_hi"), 8 * k + c // 2 * 2 + 2)
                    src = ps[:, TURN_BANKS[c // 2], (c % 2) * S:(c % 2 + 1) * S]
                    hf = hi[:, c, :].bitcast(F32)
                    if key in FOLDED:
                        i = dve.scalar_tensor_tensor(lo[:, c, :], src, gain(key, c), hf, ALU.mult, ALU.subtract)
                    elif key in MODS:
                        g = MODS[key]
                        then(dve.tensor_scalar(shifted(c), src, modA[:, g, c:c + 1], modB[:, g, c:c + 1], ALU.mult, ALU.add))
                        i = dve.tensor_tensor(lo[:, c, :], shifted(c), hf, ALU.subtract)
                    else:
                        i = dve.tensor_tensor(lo[:, c, :], src, hf, ALU.subtract)
                    i.then_inc(sem("act_lo"), 1)

            def shifted(c):
                return b_lo_f[:, (c % 2) * S:(c % 2 + 1) * S]

            def ffn_part(f):
                up, dn = ffn[f]
                for j in range(UPB):
                    w.to(up + 4 * j + 6)
                    if f == 0 and j == 0:
                        dve.wait_ge(sem("par_turned"), 1)
                        dve.tensor_copy(par[:, :, :].rearrange("p c r -> p (c r)"), ps[:, 7, 0:KC * NROW]).then_inc(sem("par_ready"), 1)
                    if j >= 1:
                        hidden_lo(f, j - 1)
                    take_mods(FFN[f], j)
                    if f < 3 and j >= 1:
                        ada_products(ADA_F * f + 2 * (j - 1), 2)
                    w.to(up + 4 * j + 8)
                    for t in range(T):
                        dve.wait_ge(sem("silu_ready"), 2 * (f * UPB + j) + t + 1)
                        if j >= 2:
                            dve.wait_ge(sem("hid_turned"), f * UPB + j - 1)
                        if f < 2:
                            i = dve.scalar_tensor_tensor(hid[:, j % 2, t, :], acc(t, j % 2)[:, HALF:], rstd[:, t:t + 1],
                                                         sg[:, j % 2, t, :], ALU.mult, ALU.mult)
                        else:
                            i = dve.tensor_tensor(hid[:, j % 2, t, :], sg[:, j % 2, t, :], acc(t, j % 2)[:, HALF:], ALU.mult)
                    i.then_inc(sem("hid_ready"), 1)
                w.to(dn + 5)
                if f < 3:
                    ada_products(ADA_F * f + 2 * (UPB - 1), 2)
                hidden_lo(f, UPB - 1)
                w.to(dn + 6)
                if f < 3:
                    ada_products(ADA_F * f + 2 * UPB, 2)
                w.to(dn + 7)
                take_mods(FFN[f], UPB + 1)
                w.to(dn + FC + 3)

            def hidden_lo(f, j):
                dve.wait_ge(sem("hid_hi_ready"), f * UPB + j + 1)
                dst, hf = (b[:, 2 * j:2 * j + 2, :].rearrange("p c n -> p (c n)") for b in (hid_lo, hid_hi))
                dve.tensor_tensor(dst, ps[:, 4 + j % 2, :], hf.bitcast(F32), ALU.subtract).then_inc(sem("hid_lo_ready"), 1)

            def ada_products(i0, n):
                for i in range(i0, i0 + n):
                    m, k = i // KC, i % KC
                    dve.wait_ge(sem(f"ada_landed{i % 3}"), 16 * (i // 3 + 1))
                    if k == 0:
                        if m == 0:
                            dve.wait_ge(sem("csil_ready"), 1)
                        if m >= 2:
                            dve.wait_ge(sem("mod_summed"), m - 1)
                        ins = dve.tensor_scalar(acc_m[:, m % 2, :], ada[:, i % 3, :], csil[:, 0:1], None, ALU.mult)
                    else:
                        dve.wait_ge(sem("ada_used"), i)
                        ins = dve.scalar_tensor_tensor(acc_m[:, m % 2, :], ada[:, i % 3, :], csil[:, k:k + 1], acc_m[:, m % 2, :],
                                                       ALU.mult, ALU.add)
                    ins.then_inc(sem("ada_used"), 1)

            def take_mods(key, j):
                for m in MOD_AT.get((key, j), ()):
                    dve.wait_ge(sem("mod_summed"), m + 1)
                    g, kind = m // 3, m % 3
                    if kind == 0:
                        i = dve.tensor_tensor(modB[:, g, :], ps[:, 6, 0:KC], par[:, :, ROW[("b_ada_2", m)]], ALU.add)
                    elif kind == 1:
                        r = ROW[("g_pre_2", g)]
                        then(dve.tensor_tensor(modA[:, g, :], ps[:, 6, 0:KC], par[:, :, ROW[("b_ada_2", m)]], ALU.add))
                        i = dve.scalar_tensor_tensor(modA[:, g, :], modA[:, g, :], 1.0, par[:, :, r], ALU.add, ALU.mult)
                    else:
                        i = dve.scalar_tensor_tensor(GT[:, g, :], ps[:, 6:8, :].rearrange("p b n -> p (b n)"),
                                                     1.0 if g == 1 else 0.5, GT[:, g, :], ALU.mult, ALU.mult)
                    i.then_inc(sem("mod_taken"), 1)

            def add_post(key):
                n = POST[key]
                dve.wait_ge(sem("pss_ready"), 2 * n + 2)
                rsqrt(prs[:, :], pss[:, :], 1.0 / D, small(rt))
                for t in range(T):
                    then(dve.scalar_tensor_tensor(h[:, t, :], wide(t), prs[:, t:t + 1], GT[:, MODS[key], :], ALU.mult, ALU.mult))
                    dve.tensor_tensor(x[:, t, :], x[:, t, :], h[:, t, :], ALU.add).then_inc(sem("x_ready"), 2)
                dve.wait_ge(sem("x_ready"), x_count[key])

            x_count = {"f2": 20, "mix2": 24, "f3": 28}

            def attention_part(m):
                prb = pr if m == 0 else pr2
                g0 = NG * m
                scale = HD ** -0.5
                for i in range(NG + 3):
                    if i < NG:
                        n, h0, nh, nk = GROUPS[i]
                        L = nk * P
                        s = st[:, i % 2, :, :]
                        dve.wait_ge(sem("scores_ready"), g0 + i + 1)
                        src = ps[:, 4 + i % 4, 0:nh * L].rearrange("p (h k) -> p h k", k=L)
                        then(dve.tensor_reduce(s[:, 0, 0:nh], src, AX, ALU.max))
                        if m == 0:
                            then(dve.scalar_tensor_tensor(s[:, 0, 0:nh], s[:, 0, 0:nh], scale, sinkb[:, h0:h0 + nh], ALU.mult, ALU.max))
                            then(dve.tensor_tensor(s[:, 4, 0:nh], sinkb[:, h0:h0 + nh], s[:, 0, 0:nh], ALU.subtract))
                        dve.tensor_scalar(s[:, 1, 0:nh], s[:, 0, 0:nh], -1.0, None, ALU.mult).then_inc(sem("bias_ready"), 1)
                    if m == 0:
                        conv(CONV_AT[-1] + CONV_G * i, CONV_AT[-1] + CONV_G * (i + 1))
                    if 1 <= i <= NG:
                        j = i - 1
                        n, h0, nh, nk = GROUPS[j]
                        L = nk * P
                        s = st[:, j % 2, :, :]
                        dve.wait_ge(sem("exp_done"), exps(m, j))
                        den = s[:, 2, 0:nh]
                        if m == 0:
                            then(dve.tensor_tensor(s[:, 2, 0:nh], s[:, 2, 0:nh], s[:, 3, 0:nh], ALU.add))
                        then(dve.reciprocal(s[:, 5, 0:nh], den))
                        v = prb[:, j % 2, 0:nh * L].rearrange("p (h k) -> p h k", k=L)
                        dve.tensor_tensor(v, v, s[:, 5, 0:nh].unsqueeze(2).to_broadcast([P, nh, L]), ALU.mult).then_inc(sem("probs_ready"), 1)
                    if i - 3 in ENDS:
                        n, g = ENDS[i - 3]
                        dve.wait_ge(sem("att_hi"), 4 * m + 2 * n + g + 1)
                        sl = (slice(None), slice(4 * g, 4 * g + 4), slice(n * P, (n + 1) * P))
                        dve.tensor_tensor(a_lo[sl], ps[:, 2 + g, :].rearrange("p (c q) -> p c q", q=P), a_hi[sl].bitcast(F32),
                                          ALU.subtract).then_inc(sem("att_lo"), 1)

            def conv(i0, i1):
                for i in range(i0, min(i1, TAPS * VC)):
                    k, c = i // VC, i % VC
                    src = uT[:, c, k:k + S]
                    if k == 0:
                        r = ROW[("dw_b", 0)]
                        ins = dve.tensor_scalar(y[:, c, :], src, par[:, c, 0:1], par[:, c, r:r + 1], ALU.mult, ALU.add)
                    else:
                        dve.wait_ge(sem("conv_step"), i - VC + 1)
                        ins = dve.scalar_tensor_tensor(y[:, c, :], src, par[:, c, k:k + 1], y[:, c, :], ALU.mult, ALU.add)
                    ins.then_inc(sem("conv_step"), 1)

            def gate_product(buf, part, done, t):
                dve.tensor_tensor(buf[:, t, part * D:(part + 1) * D], wide(t), buf[:, t, part * D:(part + 1) * D], ALU.mult)\
                   .then_inc(sem(done), 1)

            def merge(buf, done):
                for n in range(2):
                    a, b = slice(512 * n, 512 * (n + 1)), slice(D + 512 * n, D + 512 * (n + 1))
                    for t in range(T):
                        dve.tensor_tensor(buf[:, t, b], behind(t)[:, a], buf[:, t, b], ALU.mult).then_inc(sem(done), 1)
                    for t in range(T):
                        dve.wait_ge(sem(done), 2 * n + t + 1)
                        dve.tensor_tensor(buf[:, t, a], buf[:, t, a], buf[:, t, b], ALU.add).then_inc(sem("h_ready"), 1)

            dve.wait_ge(sem("const_landed"), 16)
            dve.tensor_copy(identb[:, :], ident).then_inc(sem("mask_ready"), 1)
            dve.tensor_copy(maskD[:, :], const[:, C_D:C_D + P]).then_inc(sem("mask_ready"), 1)
            dve.tensor_copy(maskWD[:, 0:P], const[:, C_W:C_W + P]).then_inc(sem("mask_ready"), 1)
            dve.tensor_copy(maskWD[:, P:], const[:, C_D:C_D + P]).then_inc(sem("mask_ready"), 1)
            turned_lo("f0")
            w.to(4)
            row_scales("f0")
            ffn_part(0)
            dve.wait_ge(used, ffn[0][1] + FC)
            add_to_x("f0", 0.5)
            w.to(ffn[0][1] + FC + 4)
            folded_norm("mix")

            M = u_mix[0]
            dve.memset(uT[:, :, 0:TAPS - 1], 0.0).then_inc(sem("uT_ready"), 1)
            for b in range(11):
                slot = [M + 4 * b + 5 + i for i in range(4)]
                w.to(slot[1])
                if b >= 5:
                    conv(CONV_AT[b - 5], (CONV_AT[b - 5] + CONV_AT[b - 4]) // 2)
                take_mods("mix", b)
                w.to(slot[3])
                if b < 4:
                    for t in range(T):
                        dve.wait_ge(sem("csg_ready"), 2 * b + t + 1)
                        if b >= 2:
                            dve.wait_ge(sem("conv_turned"), b - 1)
                        i = dve.scalar_tensor_tensor(cub[:, b % 2, t, :], acc(t, b % 2)[:, 0:HALF], rstd[:, t:t + 1],
                                                     csg[:, b % 2, t, :], ALU.mult, ALU.mult)
                    i.then_inc(sem("cub_ready"), 1)
                if b == 4:
                    dve.wait_ge(sem("uT_ready"), 5)
                if b >= 5:
                    conv((CONV_AT[b - 5] + CONV_AT[b - 4]) // 2, CONV_AT[b - 4])
                z = qkv[:, :, 0:18 * HD].rearrange("p t (h d) -> p t h d", d=HD)
                if b == 7:
                    dve.wait_ge(sem("mix_evac"), 6)
                    dve.wait_ge(sem("small_landed"), 96)
                    then(dve.tensor_tensor(qsq[:, :, :, :], z, z, ALU.mult))
                    then(dve.tensor_reduce(rt[:, 2, :].rearrange("p (t h) -> p t h", t=T), qsq[:, :, :, :], AX, ALU.add))
                    rsqrt(rs36[:, :], rt[:, 2, :], 1.0 / HD, small(rt, 36))
                if b == 8:
                    for t in range(T):
                        zt_ = z[:, t, :, :]
                        then(dve.tensor_tensor(zt_, zt_, rs36[:, 18 * t:18 * t + 18].unsqueeze(2).to_broadcast([P, 18, HD]), ALU.mult))
                        dve.tensor_tensor(zt_[:, 0:NH, :], zt_[:, 0:NH, :], gq[:, :].unsqueeze(1).to_broadcast([P, NH, HD]), ALU.mult)
                        then(dve.tensor_tensor(zt_[:, NH:, :], zt_[:, NH:, :], gk[:, :].unsqueeze(1).to_broadcast([P, 2, HD]), ALU.mult))
                if b == 9:
                    for t in range(T):
                        cos = const[:, C_COS + 8 * t:C_COS + 8 * t + 8].unsqueeze(1).to_broadcast([P, 18, 8])
                        sin = const[:, C_SIN + 8 * t:C_SIN + 8 * t + 8].unsqueeze(1).to_broadcast([P, 18, 8])
                        zt_ = z[:, t, :, :]
                        for n, (part, table) in enumerate([(0, cos), (1, sin), (1, cos), (0, sin)]):
                            i = dve.tensor_tensor(rope[:, t, n, :, :], zt_[:, :, 8 * part:8 * part + 8], table, ALU.mult)
                    then(i)
                    for t in range(T):
                        dve.tensor_tensor(z[:, t, :, 0:8], rope[:, t, 0, :, :], rope[:, t, 1, :, :], ALU.subtract)
                        i = dve.tensor_tensor(z[:, t, :, 8:16], rope[:, t, 2, :, :], rope[:, t, 3, :, :], ALU.add)
                    then(i)
                    for t in range(T):
                        for g in range(2):
                            dve.tensor_copy(kdup[:, t, g, :, :], z[:, t, NH + g, :].unsqueeze(1).to_broadcast([P, 2, HD])).then_inc(sem("qk_ready"), 1)
                if b == 10:
                    dve.memset(kTz[:, :, :, :], 0.0).then_inc(sem("kTz_cleared"), 1)
            dve.wait_ge(sem("k_turned"), 1)
            dve.wait_ge(sem("kTz_cleared"), 1)
            for g in range(2):
                for half in range(2):
                    r = slice(half * HD, (half + 1) * HD)
                    dve.tensor_copy(kTz[r, g, half, :], ps[r, 4, g * S:(g + 1) * S]).then_inc(sem("kT_ready"), 1)
            attention_part(0)
            w.to(u_ap + 5)
            dve.wait_ge(sem("conv_step"), TAPS * VC)
            dve.wait_ge(sem("y_summed"), 1)
            then(dve.tensor_scalar(lnb[:, 0, :], ps[:, 4, 0:S], 1.0 / D, None, ALU.mult))
            dve.tensor_tensor(y[:, :, :], y[:, :, :], lnb[:, 0, :].unsqueeze(1).to_broadcast([P, KC, S]), ALU.subtract)\
               .then_inc(sem("yc_ready"), 1)
            w.to(u_cp)
            dve.wait_ge(sem("y_summed"), 2)
            rsqrt(lnb[:, 1, :], ps[:, 5, 0:S], 1.0 / D, [lnt[:, 0, :], lnt[:, 1, :]])
            w.to(u_cp + 1)
            dve.tensor_tensor(y[:, :, :], y[:, :, :], lnb[:, 1, :].unsqueeze(1).to_broadcast([P, KC, S]), ALU.mult)\
               .then_inc(sem("yn_ready"), 1)
            w.to(u_cp + 2)
            for c in range(KC):
                if c % 2 == 0:
                    dve.wait_ge(sem("b_hi_ready"), c // 2 + 1)
                dve.tensor_tensor(b_lo[:, c, :], cf[:, c, :], b_hi[:, c, :].bitcast(F32), ALU.subtract).then_inc(sem("b_ready"), 1)
            w.to(u_cp + 4)
            dve.wait_ge(used, u_cp)
            for t in range(T):
                gate_product(gates, 0, "gated_a", t)
            w.to(u_wo + 3)
            dve.wait_ge(used, u_wo)
            merge(gates, "gated_b")
            w.to(u_wo + 4)
            turned_lo("merge")
            w.to(ffn[1][0] + 3)
            dve.wait_ge(used, ffn[1][0])
            add_to_x("mix", 1.0)
            w.to(ffn[1][0] + 4)
            folded_norm("f1")
            ffn_part(1)
            dve.wait_ge(sem("pin_hi"), 1)
            dve.tensor_tensor(b_lo[:, 0:2, :].rearrange("p c n -> p (c n)"), ps[:, 4, :],
                              b_hi[:, 0:2, :].rearrange("p c n -> p (c n)").bitcast(F32), ALU.subtract).then_inc(sem("pin_lo"), 1)
            dve.wait_ge(used, ffn[1][1] + FC)
            add_to_x("f1", 0.5)
            w.to(u_pp + 4)
            turned_lo("gate")
            w.to(u_pg + 4)
            row_scales("gate")
            w.to(u_pg + 6)
            dve.wait_ge(sem("pss_ready"), 2)
            dve.wait_ge(sem("grow_landed"), 16)
            rsqrt(prs[:, :], pss[:, :], 1.0 / D, small(rt))
            for t in range(T):
                dve.scalar_tensor_tensor(emb[:, t, :], wide(t), prs[:, t:t + 1], grow[:, :], ALU.mult, ALU.mult).then_inc(sem("emb_ready"), 1)
            w.to(u_pg + KC + 3)
            for t in range(T):
                dve.wait_ge(sem("gate_ready"), t + 1)
                then(dve.tensor_tensor(h[:, t, :], h[:, t, :], emb[:, t, :], ALU.mult))
                dve.tensor_tensor(x[:, t, :], x[:, t, :], h[:, t, :], ALU.add).then_inc(sem("x_ready"), 2)
            w.to(u_pg + KC + 4)
            dve.wait_ge(sem("x_ready"), 16)
            normalise("f2")
            turned_lo("f2")
            ffn_part(2)
            add_post("f2")
            w.to(ffn[2][1] + FC + 4)
            normalise("mix2")
            turned_lo("mix2")

            qf, kf, bf = (b_[:, :, :].rearrange("p h n -> p (h n)") for b_ in (qa, ka, bc))

            def masked(i):
                dve.wait_ge(sem("gla_scores"), i + 1)
                if i == NSTEP - 1:
                    dve.tensor_copy(AT[:, 2, :, :].rearrange("p h n -> p (h n)"), ps[:, 4, :]).then_inc(sem("gla_masked"), 1)
                    return
                m = glam[:, i, :].unsqueeze(1).to_broadcast([P, GH, P])
                tmp = gtmp[:, :].rearrange("p (h n) -> p h n", n=P)
                for tile in range(T):
                    src = ps[:, 4 + tile, :].rearrange("p (h n) -> p h n", n=P)
                    if i == 0:
                        ins = dve.tensor_tensor(AT[:, tile, :, :], src, m, ALU.mult)
                    else:
                        then(dve.tensor_tensor(tmp, src, m, ALU.mult))
                        ins = dve.tensor_tensor(AT[:, tile, :, :], AT[:, tile, :, :], tmp, ALU.add)
                    if tile == T - 1:
                        ins.then_inc(sem("gla_masked"), 1)
                        dve.wait_ge(sem("gla_masked"), i + 1)
                    else:
                        then(ins)

            def blocks(a, L, side):
                return a.rearrange("p (b s l) -> p b s l", s=2, l=L)[:, :, side, :]

            def level(i):
                L = (LEVELS + [P])[i - 1]
                return L, [dd[:, s, :].rearrange("p (b l) -> p b l", l=L) for s in range(2)]

            def differences(i):
                L, d = level(i)
                n = GH * S // (2 * L)
                last = bf.rearrange("p (b s l) -> p b s l", s=2, l=L)[:, :, 0, L - 1:L].to_broadcast([P, n, L])
                then(dve.tensor_tensor(d[0], blocks(bf, L, 1), last, ALU.subtract))
                dve.tensor_tensor(d[1], last, blocks(bf, L, 0), ALU.subtract).then_inc(sem("diff_ready"), 1)

            def decayed(i):
                L, d = level(i)
                dve.wait_ge(sem("decay_ready"), i)
                then(dve.tensor_tensor(blocks(qd[:, :], L, 1), blocks(qf, L, 1), d[0], ALU.mult))
                dve.tensor_tensor(blocks(kd[:, :], L, 0), blocks(kf, L, 0), d[1], ALU.mult).then_inc(sem("decayed"), 1)

            w.to(M2 + 4)
            for b in range(13):
                u1 = u_mix2[b + 1]
                if b >= 5:
                    masked(b - 5)
                    differences(b - 4)
                w.to(u1 + 2)
                if b == 1:
                    dve.wait_ge(sem("mix2_evac"), 2)
                    then(dve.tensor_tensor(lf[:, 0, :, :], sm[:, :, 16:32], bfb[:, :].unsqueeze(1).to_broadcast([P, T, NH]), ALU.add))
                    dve.scalar_tensor_tensor(lf[:, 1, :, :], lf[:, 0, :, :], -1.0, lf[:, 0, :, :], ALU.mult, ALU.min).then_inc(sem("nf_ready"), 1)
                if b == 2:
                    dve.wait_ge(sem("lnf_ready"), 1)
                    dve.scalar_tensor_tensor(lf[:, 2, :, :], lf[:, 0, :, :], 0.0, lf[:, 1, :, :], ALU.min, ALU.subtract).then_inc(sem("lf_ready"), 1)
                    dve.wait_ge(sem("decay_product"), 1)
                    for q in range(GH):
                        i = dve.tensor_scalar(ya[:, q, :], ps[:, 6 + q // 2, (q % 2) * S:(q % 2 + 1) * S], baT[:, q:q + 1], None, ALU.add)
                    then(i)
                    dve.scalar_tensor_tensor(la[:, :, :], ya[:, :, :], -1.0, ya[:, :, :], ALU.mult, ALU.min).then_inc(sem("na_ready"), 1)
                if b == 3:
                    dve.wait_ge(sem("F_summed"), 1)
                    dve.tensor_copy(Fc[:, :, :].rearrange("p t h -> p (t h)"), ps[:, 6, 0:T * NH]).then_inc(sem("F_ready"), 1)
                if b == 4:
                    dve.wait_ge(sem("lna_ready"), 1)
                    then(dve.scalar_tensor_tensor(la[:, :, :], ya[:, :, :], 0.0, la[:, :, :], ALU.min, ALU.subtract))
                    for q in range(GH):
                        dve.tensor_tensor_scan(bc[:, q, :], ones[:, 0:1].to_broadcast([P, S]), la[:, q, :], 0.0, ALU.mult, ALU.add)\
                           .then_inc(sem("bc_ready"), 1)
                    dve.wait_ge(sem("bc_ready"), GH)
                    dve.wait_ge(sem("z_turned"), 2)
                    dve.wait_ge(sem("qka_ready"), 2)
                    dve.wait_ge(sem("glam_landed"), 32)
                    then(dve.memset(qd[:, :], 0.0))
                    then(dve.memset(kd[:, :], 0.0))
                if 8 <= b <= 11:
                    dve.wait_ge(sem("z_turned"), b - 5)
                    dst = qb if b < 10 else kb
                    for i in range(2, 4):
                        h0 = 8 * (b % 2) + 2 * i
                        dve.tensor_copy(dst[:, h0:h0 + 2, :].rearrange("p h n -> p (h n)"), ps[0:AUG, 4 + i, :]).then_inc(sem("qkb_dve"), 1)
                if b >= 5:
                    decayed(b - 4)
                w.to(u1 + 4)
                if 7 <= b <= 10:
                    dve.wait_ge(sem("z_turned"), b - 5)
                    if b == 7:
                        dve.wait_ge(sem("F_ready"), 1)
                    f = Fc[:, :, 8 * ((b - 7) % 2):8 * ((b - 7) % 2) + 8]
                    one, col, sign = (HD, HD + 1, 1.0) if b < 9 else (HD + 1, HD, -1.0)
                    dve.memset(aug[:, :, :, one], 1.0).then_inc(sem("aug_ready"), 1)
                    dve.tensor_scalar(aug[:, :, :, col], f, sign, None, ALU.mult).then_inc(sem("aug_ready"), 1)

            masked(NSTEP - 1)
            dve.wait_ge(sem("gla_squares"), T * GH)
            rsqrt(ga_ss[:, 1, :], ga_ss[:, 0, :], 1.0 / GDV, [ga_ss[:, 2, :], ga_ss[:, 3, :]])
            for t in range(T):
                for q in range(GH):
                    c = slice(q * GDV, (q + 1) * GDV)
                    i = dve.scalar_tensor_tensor(va[:, t, c], ps[:, 4 + 2 * t + q // 2, (q % 2) * GDV:(q % 2 + 1) * GDV],
                                                 ga_ss[:, 1, t * GH + q:t * GH + q + 1], ggla[:, c], ALU.mult, ALU.mult)
                then(i)
            for n in range(2):
                for t in range(T):
                    c = slice(512 * n, 512 * (n + 1))
                    dve.tensor_tensor(va[:, t, c], va[:, t, c], ra[:, t, c], ALU.mult).then_inc(sem("h_ready"), 1)
            G = u_mix2[13]
            w.to(G + 8)
            w.to(G + 12)
            turned_lo("oa", b_hi, b_lo)
            w.to(G + 20)
            attention_part(1)
            w.to(u_pb + 4)
            dve.wait_ge(used, u_pb)
            for t in range(T):
                gate_product(gates2, 0, "gated2_a", t)
            w.to(u_wo2 + 3)
            dve.wait_ge(used, u_wo2)
            merge(gates2, "gated2_b")
            w.to(u_wo2 + 4)
            turned_lo("merge2")
            w.to(u_wo2 + KC + 3)
            add_post("mix2")
            w.to(u_wo2 + KC + 4)
            normalise("f3")
            turned_lo("f3")
            ffn_part(3)
            add_post("f3")

        @block.tensor
        def _(pe):
            def slot(u, buf, kk, n, c0=0, c1=None):
                a = buf[:, u % SPLIT, kk * n:(kk + 1) * n]
                return a[:, c0:c1 if c1 is not None else n]

            def col_unit(u, k0, dst, hi=a_hi, lo=a_lo):
                _, nk, n = units[u]
                pe.wait_ge(lo_ready, u + 1)
                for kk in range(nk):
                    kc = k0 + kk
                    for t in range(T):
                        a = [v[:, kc, t * P:(t + 1) * P] for v in (hi, lo)]
                        pe.matmul(dst(t)[:, 0:n], a[0], slot(u, w_hi, kk, n), start=kc == 0, stop=False)
                        pe.matmul(dst(t)[:, 0:n], a[0], slot(u, w_lo, kk, n), start=False, stop=False)
                        i = pe.matmul(dst(t)[:, 0:n], a[1], slot(u, w_hi, kk, n), start=False, stop=kc == KC - 1)
                i.then_inc(used, 1)

            def row_unit(u, kc, last, hi, lo, bank=0, early=False):
                pe.wait_ge(lo_ready, u + 1)
                for t in range(T):
                    a = [v[:, kc, t * P:(t + 1) * P] for v in (hi, lo)]
                    for x_, w_ in ((0, w_hi), (0, w_lo), (1, w_hi)):
                        for n in range(2):
                            i = pe.matmul(ps[:, bank + 2 * t + n, :], a[x_], slot(u, w_, 0, D, 512 * n, 512 * (n + 1)),
                                          start=kc == 0 and x_ == 0 and w_ is w_hi, stop=kc == last and x_ == 1)
                    if t == 0 and early:
                        i.then_inc(sem("first_tile"), 1)
                i.then_inc(used, 1)

            def turn(key, src):
                for b in range(4):
                    if key in MADE and b % 2 == 0:
                        pe.wait_ge(sem("h_ready"), 4 * MADE[key] + b + 2)
                    if key in FOLDED and key != "f0" and b % 2 == 0:
                        pe.wait_ge(sem("x_ready"), 4 * (NORM[key] - 1) + b + 2)
                    for c in range(2 * b, 2 * b + 2):
                        for t in range(T):
                            i = pe.transpose(ps[:, TURN_BANKS[b], (c % 2) * S + t * P:(c % 2) * S + (t + 1) * P], src[:, t, c * P:(c + 1) * P], ident)
                    i.then_inc(sem("turned"), 1)

            def act_ready(key, kc):
                pe.wait_ge(sem("act_lo"), 8 * TURN[key] + kc + 1)

            def ffn_part(f):
                up, dn = ffn[f]
                for j in range(UPB):
                    if j >= 2:
                        pe.wait_ge(sem("hid_ready"), f * UPB + j - 1)
                    for i in range(4):
                        if j == 0:
                            act_ready(FFN[f], 2 * i + 1)
                        col_unit(up + 4 * j + i, 2 * i, lambda t: acc(t, j % 2))
                        if i == 1:
                            if f == 0 and j == 0:
                                pe.wait_ge(sem("prow_landed"), 16 * (5 + len(ONE_ROW)))
                                for c in range(KC):
                                    ins = pe.transpose(ps[:, 7, c * NROW:(c + 1) * NROW], prow[:, c * P:(c + 1) * P], ident[0:NROW, 0:NROW])
                                ins.then_inc(sem("par_turned"), 1)
                            if j >= 1:
                                turn_hidden(f, j - 1)
                            sum_mods(FFN[f], j)
                for k in range(FC):
                    if k == 2:
                        turn_hidden(f, UPB - 1)
                    if f == 1 and k == 8:
                        pe.wait_ge(sem("pin_landed"), 16)
                        pe.wait_ge(sem("hid_lo_ready"), f * UPB + UPB)
                        for c in range(2):
                            for t in range(T):
                                i = pe.transpose(ps[:, 4, c * S + t * P:c * S + (t + 1) * P], pin[:, t, c * P:(c + 1) * P], ident)
                        i.then_inc(sem("pin_turned"), 1)
                    pe.wait_ge(sem("hid_lo_ready"), f * UPB + k // 2 + 1)
                    if k == 0:
                        first_down(f, dn)
                        continue
                    row_unit(dn + k, k, FC - 1, hid_hi, hid_lo, early=f >= 2 and k == FC - 1)
                    if k == 3:
                        sum_mods(FFN[f], UPB + 1)

            def first_down(f, u):
                pe.wait_ge(lo_ready, u + 1)
                for n in (1, 0):
                    if n == 0:
                        pe.wait_ge(sem("hid_ready"), f * UPB + UPB)
                    for t in range(T):
                        a = [v[:, 0, t * P:(t + 1) * P] for v in (hid_hi, hid_lo)]
                        for x_, w_ in ((0, w_hi), (0, w_lo), (1, w_hi)):
                            i = pe.matmul(ps[:, 2 * t + n, :], a[x_], slot(u, w_, 0, D, 512 * n, 512 * (n + 1)),
                                          start=x_ == 0 and w_ is w_hi, stop=False)
                i.then_inc(used, 1)

            def turn_hidden(f, j):
                pe.wait_ge(sem("hid_ready"), f * UPB + j + 1)
                if j >= 2:
                    pe.wait_ge(sem("hid_lo_ready"), f * UPB + j - 1)
                for c in range(2):
                    for t in range(T):
                        i = pe.transpose(ps[:, 4 + j % 2, c * S + t * P:c * S + (t + 1) * P], hid[:, j % 2, t, c * P:(c + 1) * P], ident)
                i.then_inc(sem("hid_turned"), 1)

            def sum_mods(key, j):
                for m in MOD_AT.get((key, j), ()):
                    pe.wait_ge(sem("ada_used"), KC * (m + 1))
                    if m >= 1:
                        pe.wait_ge(sem("mod_taken"), m)
                    if m % 3 == 2:
                        if m == 2:
                            pe.wait_ge(sem("gpost_landed"), 96)
                        for n in range(2):
                            c = slice(512 * n, 512 * (n + 1))
                            pe.matmul(ps[:, 6 + n, :], ones, acc_m[:, m % 2, c], start=True, stop=False)
                            i = pe.matmul(ps[:, 6 + n, :], ident[0:3, m // 3:m // 3 + 1].to_broadcast([3, P]), brow[:, c], start=False, stop=True)
                    else:
                        for c in range(KC):
                            i = pe.matmul(ps[:, 6, c:c + 1], acc_m[:, m % 2, c * P:(c + 1) * P], ones[:, 0:1], start=True, stop=True)
                    i.then_inc(sem("mod_summed"), 1)

            def attention_part(m):
                prb, ptb = (pr, pt) if m == 0 else (pr2, pt2)
                g0 = NG * m

                def scores(i):
                    n, h0, nh, nk = GROUPS[i]
                    L = nk * P
                    bank = ps[:, 4 + i % 4, :]
                    if i >= 4:
                        pe.wait_ge(sem("exp_done"), exps(m, i - 4))
                    if m == 0:
                        mask = maskD[:, :] if n == 0 else maskWD[:, :]
                        pe.matmul(bank.rearrange("p (h k) -> p h k", k=L), identb[:, :], mask.unsqueeze(1).to_broadcast([P, nh, L]),
                                  start=True, stop=True)
                    else:
                        v = bank.rearrange("p (h k) -> p h k", k=L)[:, :, (nk - 1) * P:]
                        pe.matmul(v, identb[:, :], maskD[:, :].unsqueeze(1).to_broadcast([P, nh, P]), start=True, stop=True,
                                  skip_group_check=True)
                    for q in range(nh):
                        hh = h0 + q
                        if m == 0:
                            lhs, rhs = qT[:, hh // 2, n * P:(n + 1) * P], kTz[:, hh // 8, hh % 2, 0:L]
                        else:
                            lhs, rhs = qb[:, hh, n * P:(n + 1) * P], kb[:, hh, 0:L]
                        i_ = pe.matmul(bank[:, q * L:(q + 1) * L], lhs, rhs, start=False, stop=True, skip_group_check=True)
                    i_.then_inc(sem("scores_ready"), 1)

                def turn_probs(i):
                    pe.wait_ge(sem("probs_ready"), g0 + i + 1)
                    if i >= 2:
                        pe.wait_ge(sem("pt_ready"), g0 + i - 1)
                    for q in range(4):
                        i_ = pe.transpose(ps[:, i % 2, q * P:(q + 1) * P], prb[:, i % 2, q * P:(q + 1) * P], ident)
                    i_.then_inc(sem("probs_turned"), 1)

                def values(i):
                    n, h0, nh, nk = GROUPS[i]
                    pe.wait_ge(sem("pt_ready"), g0 + i + 1)
                    if n == 1 and h0 in (0, 8):
                        pe.wait_ge(sem("att_lo"), 4 * m + h0 // 8 + 1)
                    for q in range(nh):
                        hh = h0 + q
                        r = (hh % 2) * HD
                        dst = ps[r:r + HD, 2 + hh // 8, (hh % 8 // 2) * P:(hh % 8 // 2 + 1) * P]
                        for k in range(nk):
                            if m == 0:
                                v = qkv[:, k, 18 * HD + (hh // 8) * HD:18 * HD + (hh // 8 + 1) * HD]
                            else:
                                v = vb[:, k, hh * HD:(hh + 1) * HD]
                            c = (q * nk + k) * P
                            i_ = pe.matmul(dst, v, ptb[:, i % 2, c:c + P], start=k == 0, stop=k == nk - 1)
                    i_.then_inc(sem("values_done"), 1)

                for i in range(NG + 3):
                    if i < NG:
                        scores(i)
                    if 2 <= i < NG + 2:
                        turn_probs(i - 2)
                    if i >= 3:
                        values(i - 3)

            pe.wait_ge(sem("const_landed"), 16)
            pe.wait_ge(sem("x_landed"), 16)
            turn("f0", x)
            ffn_part(0)
            turn("mix", x)

            M = u_mix[0]
            for b in range(11):
                if 2 <= b < 6:
                    pe.wait_ge(sem("cub_ready"), b - 1)
                elif b >= 6:
                    pe.wait_ge(sem("mix_evac"), 2 * (b - 5))
                for i in range(4):
                    if b == 0:
                        act_ready("mix", 2 * i + 1)
                    col_unit(M + 4 * b + i, 2 * i, lambda t: acc(t, b % 2))
                    if i == 1:
                        if 1 <= b <= 4:
                            j = b - 1
                            pe.wait_ge(sem("cub_ready"), j + 1)
                            if j >= 2:
                                pe.wait_ge(sem("uT_ready"), j - 1)
                            for c in range(2):
                                for t in range(T):
                                    ins = pe.transpose(ps[:, 4 + j % 2, c * S + t * P:c * S + (t + 1) * P],
                                                       cub[:, j % 2, t, c * P:(c + 1) * P], ident)
                            ins.then_inc(sem("conv_turned"), 1)
                        if b == 10:
                            pe.wait_ge(sem("qk_ready"), 4)
                            for j in range(4):
                                for c in range(2 * j, 2 * j + 2):
                                    for t in range(T):
                                        ins = pe.transpose(ps[:, 4 + j, (c % 2) * S + t * P:(c % 2) * S + (t + 1) * P],
                                                           qkv[:, t, c * P:(c + 1) * P], ident)
                                ins.then_inc(sem("q_turned"), 1)
            pe.wait_ge(sem("qT_ready"), 1)
            for g in range(2):
                for t in range(T):
                    i = pe.transpose(ps[:, 4, g * S + t * P:g * S + (t + 1) * P], kdup[:, t, g, :, :].rearrange("p a d -> p (a d)"), ident)
            i.then_inc(sem("k_turned"), 1)
            pe.wait_ge(sem("mix_evac"), 14)
            pe.wait_ge(sem("kT_ready"), 4)
            pe.wait_ge(sem("qT_ready"), 4)
            pe.wait_ge(sem("mask_ready"), 4)
            attention_part(0)
            pe.wait_ge(sem("att_lo"), 4)
            for k in range(KC):
                row_unit(u_ap + k, k, KC - 1, a_hi, a_lo)
                if k == 0:
                    pe.wait_ge(sem("conv_step"), TAPS * VC)
                    pe.wait_ge(sem("pool_step"), POOLC * (TAPS - 1))
                    for c in range(KC):
                        i = pe.matmul(ps[:, 4, 0:S], ones, y[:, c, :], start=c == 0, stop=c == KC - 1)
                    i.then_inc(sem("y_summed"), 1)
                if k == 3:
                    pe.wait_ge(sem("ysq_ready"), 1)
                    for c in range(KC):
                        i = pe.matmul(ps[:, 5, 0:S], ones, ysq[:, c, :], start=c == 0, stop=c == KC - 1)
                    i.then_inc(sem("y_summed"), 1)
            for k in range(KC):
                pe.wait_ge(sem("b_ready"), k + 1)
                row_unit(u_cp + k, k, KC - 1, b_hi, b_lo, bank=4)
            pe.wait_ge(sem("gated_a"), 2)
            turn("merge", gates)
            for k in range(KC):
                act_ready("merge", k)
                row_unit(u_wo + k, k, KC - 1, a_hi, a_lo)
            turn("f1", x)
            ffn_part(1)
            turn("gate", x)
            for k in range(2):
                row_unit(u_pp + k, k, 1, b_hi, b_lo)
            act_ready("gate", KC - 1)
            for k in range(KC):
                row_unit(u_pg + k, k, KC - 1, a_hi, a_lo, bank=4, early=k == KC - 1)
            turn("f2", h)
            ffn_part(2)
            turn("mix2", h)

            def gla_scores(i):
                if i >= 1:
                    pe.wait_ge(sem("decayed"), i)
                if i == NSTEP - 1:
                    for q in range(GH):
                        ins = pe.matmul(ps[:, 4, q * P:(q + 1) * P], kd[:, q * S:q * S + P], qd[:, q * S + P:(q + 1) * S], start=True, stop=True)
                else:
                    for tile in range(T):
                        for q in range(GH):
                            c = slice(q * S + tile * P, q * S + (tile + 1) * P)
                            if i == 0:
                                k_, q_ = (v[:, q, tile * P:(tile + 1) * P] for v in (ka, qa))
                            else:
                                k_, q_ = kd[:, c], qd[:, c]
                            ins = pe.matmul(ps[:, 4 + tile, q * P:(q + 1) * P], k_, q_, start=True, stop=True)
                ins.then_inc(sem("gla_scores"), 1)

            for b in range(13):
                u0 = u_mix2[b]
                if b >= 2:
                    pe.wait_ge(sem("mix2_evac"), 2 * (b - 1))
                if b == 0:
                    act_ready("mix2", KC - 1)
                    col_unit(u0, 0, lambda t: acc(t, 0))
                    continue
                for i in range(4):
                    col_unit(u0 + i, 2 * i, lambda t: acc(t, b % 2))
                    if i != 1:
                        continue
                    if b == 1:
                        pe.wait_ge(sem("mix2_evac"), 2)
                        for t in range(T):
                            ins = pe.transpose(ps[0:16, 6, t * P:(t + 1) * P], sm[:, t, 0:16], ident)
                        ins.then_inc(sem("alow_turned"), 1)
                    if b in (2, 3):
                        pe.wait_ge(sem("mix2_evac"), 2 * b)
                        if b == 3:
                            pe.wait_ge(sem("qka_ready"), 1)
                        for q in range(GH):
                            for t in range(T):
                                ins = pe.transpose(ps[:, 4 + q // 2, (q % 2) * S + t * P:(q % 2) * S + (t + 1) * P],
                                                   zt[:, t, q * P:(q + 1) * P], ident)
                        ins.then_inc(sem("z_turned"), 1)
                    if b == 2:
                        pe.wait_ge(sem("alT_ready"), 1)
                        for q in range(GH):
                            ins = pe.matmul(ps[:, 6 + q // 2, (q % 2) * S:(q % 2 + 1) * S], wa2[:, q * P:(q + 1) * P], alT[:, :],
                                            start=True, stop=True)
                        ins.then_inc(sem("decay_product"), 1)
                    if b == 3:
                        pe.wait_ge(sem("lf_ready"), 1)
                        pe.wait_ge(sem("na_ready"), 1)
                        tri = const[:, C_TRI:C_TRI + P]
                        pe.matmul(ps[:, 6, 0:NH], tri, lf[:, 2, 0, :], start=True, stop=True)
                        pe.matmul(ps[:, 6, NH:2 * NH], ones, lf[:, 2, 0, :], start=True, stop=False)
                        pe.matmul(ps[:, 6, NH:2 * NH], tri, lf[:, 2, 1, :], start=False, stop=True).then_inc(sem("F_summed"), 1)
                    if 8 <= b <= 11:
                        pe.wait_ge(sem("mix2_evac"), 2 * b)
                        pe.wait_ge(sem("aug_ready"), 2 * (b - 7))
                        if b == 8:
                            pe.wait_ge(sem("qka_ready"), 2)
                            pe.wait_ge(sem("F_ready"), 1)
                        else:
                            pe.wait_ge(sem("qkb_act"), 2 * (b - 8))
                            pe.wait_ge(sem("qkb_dve"), 2 * (b - 8))
                        pe.wait_ge(sem("gla_masked"), b - 4)
                        for q in range(8):
                            for t in range(T):
                                ins = pe.transpose(ps[0:AUG, 4 + q // 2, (q % 2) * S + t * P:(q % 2) * S + (t + 1) * P],
                                                   aug[:, t, q, :], ident)
                        ins.then_inc(sem("z_turned"), 1)
                if b >= 4:
                    if b == 4:
                        pe.wait_ge(sem("qka_ready"), 2)
                    if b >= 5:
                        pe.wait_ge(sem("gla_masked"), b - 4)
                    if 8 <= b <= 11:
                        pe.wait_ge(sem("qkb_act"), 2 * (b - 7))
                    gla_scores(b - 4)

            pe.wait_ge(sem("gla_masked"), NSTEP)
            pe.wait_ge(sem("qkb_dve"), 8)
            for t in range(T):
                for q in range(GH):
                    dst = ps[:, 4 + 2 * t + q // 2, (q % 2) * GDV:(q % 2 + 1) * GDV]
                    v = [va[:, s, q * GDV:(q + 1) * GDV] for s in range(T)]
                    if t == 0:
                        ins = pe.matmul(dst, AT[:, 0, q, :], v[0], start=True, stop=True)
                    else:
                        pe.matmul(dst, AT[:, 2, q, :], v[0], start=True, stop=False)
                        ins = pe.matmul(dst, AT[:, 1, q, :], v[1], start=False, stop=True)
                ins.then_inc(sem("gla_out"), 1)
            G = u_mix2[13]
            for b in range(4):
                if b == 0:
                    pe.wait_ge(sem("mix2_evac"), 26)
                if b >= 2:
                    pe.wait_ge(sem("gates2_ready"), 2 * (b - 1))
                for i in range(4):
                    col_unit(G + 4 * b + i, 2 * i, lambda t: acc(t, b % 2))
                    if b == 1 and i == 1:
                        turn("oa", va)
            pe.wait_ge(sem("gates2_ready"), 8)
            pe.wait_ge(sem("act_lo"), 8 * TURN["oa"] + 8)
            attention_part(1)
            pe.wait_ge(sem("att_lo"), 8)
            for k in range(KC):
                row_unit(u_pa + k, k, KC - 1, b_hi, b_lo)
            for k in range(KC):
                row_unit(u_pb + k, k, KC - 1, a_hi, a_lo, bank=4)
            pe.wait_ge(sem("gated2_a"), 2)
            turn("merge2", gates2)
            for k in range(KC):
                act_ready("merge2", k)
                row_unit(u_wo2 + k, k, KC - 1, a_hi, a_lo, early=k == KC - 1)
            turn("f3", h)
            ffn_part(3)


_INS = ["x", "p", "ffn1_norm", "ffn1_wgu", "ffn1_wdown", "mix_norm", "w_in", "q_norm", "k_norm", "sinks", "attn_proj",
        "dw_w", "dw_b", "conv_ln_g", "conv_ln_b", "conv_proj", "w_out", "ffn2_norm", "ffn2_wgu", "ffn2_wdown",
        "ple_proj", "ple_norm", "ple_gate_norm", "ple_gate_w", "c_2", "w_ada_2", "b_ada_2", "g_pre_2", "g_post_2",
        "w_gu1_2", "w_dn1_2", "w_gu2_2", "w_dn2_2", "w_in_2", "w_a2_2", "b_a_2", "b_f_2", "g_gla_2", "w_pa_2", "w_pb_2",
        "w_out_2"]


def kernel(**inputs):
    import numpy as _np
    import concourse.bacc as _bacc
    from concourse import mybir as _mybir
    from concourse.bass_utils import run_bass_kernel_spmd as _run

    nc = _bacc.Bacc("TRN2", target_bir_lowering=False, num_devices=1)
    arrays, args = {}, {}
    for name in _INS:
        a = _np.ascontiguousarray(inputs[name])
        arrays[f"in_{name}_dram"] = a
        args[name] = nc.dram_tensor(f"in_{name}_dram", a.shape, _mybir.dt.from_np(a.dtype), kind="ExternalInput").ap()
    table = shape_constants()
    arrays["shape_constants_dram"] = table
    consts = nc.dram_tensor("shape_constants_dram", table.shape, _mybir.dt.float32, kind="ExternalInput").ap()
    out = nc.dram_tensor("out_0_dram", (1, S, D), _mybir.dt.float32, kind="ExternalOutput").ap()
    two_blocks(nc, args, consts, out)
    r = _run(nc, [arrays], core_ids=[0])
    return r.results[0]["out_0_dram"]
```
